# Optimizing a Trainium2 kernel written in Bass

```python
import jax, jax.numpy as jnp
from jax import lax
import numpy as np

D_MODEL = 2048
BATCH = 1
SEQ = 256
DEPTH = 2

N_MIXERS = 2
N_HEADS = 16
HEAD_DIM = D_MODEL // N_HEADS
D_FF = 4 * D_MODEL
CONV_WIDTH = 3
Q_BLOCK = 128
N_ATTN_LAYERS = (DEPTH + 1) // 2
N_CONV_LAYERS = DEPTH // 2
N_MOD = 6
DEEPNORM_ALPHA = (2.0 * DEPTH) ** 0.25
DEEPNORM_BETA = (8.0 * DEPTH) ** -0.25
LN_EPS = 1e-5
MOD_INIT_SCALE = 0.1

kernel_name = "hybrid_stickbreak_shortconv_deepnorm_adaln"

def layer_norm(x, g, b):
    xf = x.astype(jnp.float32)
    mu = jnp.mean(xf, axis=-1, keepdims=True)
    xc = xf - mu
    var = jnp.mean(xc * xc, axis=-1, keepdims=True)
    y = xc * lax.rsqrt(var + LN_EPS)
    return (y * g.astype(jnp.float32) + b.astype(jnp.float32)).astype(x.dtype)

def stick_breaking_attention(h, w_qkv, w_o):
    bsz, seq, _ = h.shape
    qkv = h @ w_qkv
    q, k, v = jnp.split(qkv, 3, axis=-1)
    q = q.reshape(bsz, seq, N_HEADS, HEAD_DIM)
    k = k.reshape(bsz, seq, N_HEADS, HEAD_DIM)
    v = v.reshape(bsz, seq, N_HEADS, HEAD_DIM)
    scale = HEAD_DIM ** -0.5
    outs = []
    for blk in range(seq // Q_BLOCK):
        start = blk * Q_BLOCK
        end = start + Q_BLOCK
        qb = q[:, start:end].astype(jnp.float32)
        kb = k[:, :end].astype(jnp.float32)
        vb = v[:, :end].astype(jnp.float32)
        z = jnp.einsum('bqhd,bkhd->bhqk', qb, kb) * scale
        t_idx = start + jnp.arange(Q_BLOCK)[:, None]
        s_idx = jnp.arange(end)[None, :]
        causal = s_idx < t_idx
        log_beta = jax.nn.log_sigmoid(z)
        log_1m = jnp.where(causal, jax.nn.log_sigmoid(-z), 0.0)
        log_stick = lax.cumsum(log_1m, axis=3, reverse=True) - log_1m
        a = jnp.where(causal, jnp.exp(log_beta + log_stick), 0.0)
        outs.append(jnp.einsum('bhqk,bkhd->bqhd', a, vb))
    o = jnp.concatenate(outs, axis=1).reshape(bsz, seq, D_MODEL).astype(h.dtype)
    return o @ w_o

def short_conv_mixer(h, w_in, conv_w, conv_b, w_out):
    bcu = h @ w_in
    b_gate, c_gate, u = jnp.split(bcu, 3, axis=-1)
    gated = c_gate * u
    y = lax.conv_general_dilated(
        gated, conv_w[:, None, :].astype(gated.dtype),
        window_strides=(1,), padding=[(CONV_WIDTH - 1, 0)],
        dimension_numbers=('NWC', 'WIO', 'NWC'),
        feature_group_count=D_MODEL) + conv_b
    return (b_gate * y) @ w_out

def sq_relu_mlp(h, w1, b1, w2, b2):
    return jnp.square(jax.nn.relu(h @ w1 + b1)) @ w2 + b2

def setup_inputs(seed: int = 0) -> dict:
    key = jax.random.key(seed)
    ks = jax.random.split(key, 20)
    d, f = D_MODEL, D_FF
    nrm = jax.random.normal
    x = nrm(ks[0], (BATCH, SEQ, d), jnp.float32)
    c = nrm(ks[1], (BATCH, d), jnp.float32)
    mod_w = nrm(ks[2], (DEPTH, d, N_MOD * d), jnp.float32) * (d ** -0.5) * MOD_INIT_SCALE
    mod_b = nrm(ks[3], (DEPTH, N_MOD * d), jnp.float32) * 0.01
    ln_g = 1.0 + 0.02 * nrm(ks[4], (DEPTH, 2, d), jnp.float32)
    ln_b = 0.02 * nrm(ks[5], (DEPTH, 2, d), jnp.float32)
    v_col_scale = jnp.concatenate([jnp.ones((2 * d,), jnp.float32),
                                   jnp.full((d,), DEEPNORM_BETA, jnp.float32)])
    attn_w_qkv = nrm(ks[6], (N_ATTN_LAYERS, d, 3 * d), jnp.float32) * (d ** -0.5) * v_col_scale
    attn_w_o = nrm(ks[7], (N_ATTN_LAYERS, d, d), jnp.float32) * (d ** -0.5) * DEEPNORM_BETA
    conv_w_in = nrm(ks[8], (N_CONV_LAYERS, d, 3 * d), jnp.float32) * (d ** -0.5)
    conv_w = nrm(ks[9], (N_CONV_LAYERS, CONV_WIDTH, d), jnp.float32) * (CONV_WIDTH ** -0.5)
    conv_b = nrm(ks[10], (N_CONV_LAYERS, d), jnp.float32) * 0.01
    conv_w_out = nrm(ks[11], (N_CONV_LAYERS, d, d), jnp.float32) * (d ** -0.5) * DEEPNORM_BETA
    mlp_w1 = nrm(ks[12], (DEPTH, d, f), jnp.float32) * (d ** -0.5) * DEEPNORM_BETA
    mlp_b1 = nrm(ks[13], (DEPTH, f), jnp.float32) * 0.01
    mlp_w2 = nrm(ks[14], (DEPTH, f, d), jnp.float32) * (f ** -0.5) * DEEPNORM_BETA
    mlp_b2 = nrm(ks[15], (DEPTH, d), jnp.float32) * 0.01
    return {"x": x, "c": c, "mod_w": mod_w, "mod_b": mod_b, "ln_g": ln_g, "ln_b": ln_b,
            "attn_w_qkv": attn_w_qkv, "attn_w_o": attn_w_o,
            "conv_w_in": conv_w_in, "conv_w": conv_w, "conv_b": conv_b, "conv_w_out": conv_w_out,
            "mlp_w1": mlp_w1, "mlp_b1": mlp_b1, "mlp_w2": mlp_w2, "mlp_b2": mlp_b2}

def reference(x, c, mod_w, mod_b, ln_g, ln_b, attn_w_qkv, attn_w_o,
              conv_w_in, conv_w, conv_b, conv_w_out, mlp_w1, mlp_b1, mlp_w2, mlp_b2):
    cond = jax.nn.silu(c)
    for i in range(DEPTH):
        mod = (cond @ mod_w[i] + mod_b[i])[:, None, :]
        sh_m, sc_m, g_m, sh_f, sc_f, g_f = jnp.split(mod, N_MOD, axis=-1)
        h = x * (1.0 + sc_m) + sh_m
        if i % N_MIXERS == 0:
            j = i // N_MIXERS
            y = stick_breaking_attention(h, attn_w_qkv[j], attn_w_o[j])
        else:
            j = i // N_MIXERS
            y = short_conv_mixer(h, conv_w_in[j], conv_w[j], conv_b[j], conv_w_out[j])
        x = layer_norm(DEEPNORM_ALPHA * x + (1.0 + g_m) * y, ln_g[i, 0], ln_b[i, 0])
        h = x * (1.0 + sc_f) + sh_f
        y = sq_relu_mlp(h, mlp_w1[i], mlp_b1[i], mlp_w2[i], mlp_b2[i])
        x = layer_norm(DEEPNORM_ALPHA * x + (1.0 + g_f) * y, ln_g[i, 1], ln_b[i, 1])
    return x


_drawn_inputs = setup_inputs


def setup_inputs(seed=0):
    import zlib

    import numpy as np

    out = dict(_drawn_inputs(seed))
    spreads = {}
    factors = {'mod_b': 5.646, 'conv_b': 8.0, 'mlp_b1': 8.0, 'mlp_b2': 5.372}
    for name, (base, spread) in spreads.items():
        noise = np.random.default_rng([zlib.crc32(name.encode()), seed]).standard_normal(out[name].shape)
        drawn = base * np.exp(spread * noise) if base else spread * noise
        out[name] = __import__('jax').numpy.asarray(drawn.astype(out[name].dtype))
    for name, factor in factors.items():
        out[name] = (out[name] * factor).astype(out[name].dtype)
    return out
```

```python
from contextlib import ExitStack

import numpy as np
import concourse.bass as bass
from concourse import mybir

F32 = mybir.dt.float32
F32R = mybir.dt.float32r
ALU = mybir.AluOpType
ACT = mybir.ActivationFunctionType
ds = bass.ds

P = 128
CREDIT_RAW = 8
CREDIT_SPLIT = 4
CREDIT_BANKS = 2
CREDIT_STAGE = 2
SHIFT_M, SCALE_M, GATE_M, SHIFT_F, SCALE_F, GATE_F = range(6)


def build_trunk(nc, x, c, mod_w, mod_b, ln_g, ln_b, attn_w_qkv, attn_w_o,
                conv_w_in, conv_w, conv_b, conv_w_out, mlp_w1, mlp_b1, mlp_w2, mlp_b2, out):
    _, T, D = x.shape
    DEPTH = mod_w.shape[0]
    FF = mlp_w1.shape[2]
    KT = D // P
    TT = T // P
    HEADS = KT
    GC = 512
    GT = GC // P
    NCH = 8
    CK = KT // NCH
    NG = D // GC
    FC = FF // D
    SLOTS = 4
    ALPHA = (2.0 * DEPTH) ** 0.25
    EPS = 1e-5
    ZSCALE = float(P) ** -0.5
    assert DEPTH == 2 and T == 2 * P and KT == 16 and conv_w.shape[1] == 3

    W_QK = 0
    W_V = W_QK + 2 * NG
    W_O = W_V + NG
    W_MLP = [W_O + NG, 0]
    W_CIN = W_MLP[0] + 2 * NG * FC
    W_COUT = W_CIN + 3 * NG
    W_MLP[1] = W_COUT + NG
    W_END = W_MLP[1] + 2 * NG * FC
    S_CONV = 2 * NG * FC - NG
    S_MLP = [0, S_CONV + 2 * NG]
    OPEN = 2
    QUARTERS = KT // GT
    QM = 2 * NCH
    QW = OPEN * NCH // QUARTERS
    QC = QM + QW
    PRE = QUARTERS * QC // NCH - OPEN
    MC0 = QUARTERS * QM
    MD0 = 2 * QUARTERS
    M_ATTN = 0
    M_MLP = [4 * NG, 0]
    M_CONV = M_MLP[0] + 2 * NG * FC
    M_MLP[1] = M_CONV + 4 * NG
    MODT = 6 * KT
    STRIP_ATTN = 3 * KT // (4 * NG)
    STRIP_W1 = KT // (NG * FC)
    STRIP_W2 = 3 * KT // (NG * FC)
    STRIP_CONV = 2 * KT // (4 * NG)
    STRIP_MAX = max(STRIP_ATTN, STRIP_W1, STRIP_W2, STRIP_CONV) * P
    SUBS = 4
    SK = KT // SUBS

    V_C, V_MODB, V_LNG = 0, KT, KT + DEPTH * MODT
    V_LNB = V_LNG + 2 * DEPTH * KT
    V_CW = V_LNB + 2 * DEPTH * KT
    V_CB = V_CW + 3 * KT
    V_B2 = V_CB + KT
    V_B1 = V_B2 + DEPTH * KT
    V_ALL = V_B1 + DEPTH * FF // P

    ctx = ExitStack()
    with ctx:
        def sb(name, shape, dt=F32):
            return ctx.enter_context(nc.sbuf_tensor(name, shape, dt))

        def sem(name):
            return ctx.enter_context(nc.semaphore(name))

        with ExitStack() as early:
            q_t = early.enter_context(nc.sbuf_tensor("q_t", [P, KT, T], F32))
            k_t = early.enter_context(nc.sbuf_tensor("k_t", [P, KT, T], F32))
            v_tok = early.enter_context(nc.sbuf_tensor("v_tok", [P, TT, D], F32))
        hid_high = sb("hid_high", [P, KT, T], F32R)
        hid_low = sb("hid_low", [P, KT, T], F32R)
        y = sb("y", [P, KT, T])
        tok = q_t[:, :, :].rearrange("p k t -> p (k t)").rearrange("p (t d) -> p t d", t=TT)

        res = sb("res", [P, KT, T])
        h_high = sb("h_high", [P, KT, T], F32R)
        h_low = sb("h_low", [P, KT, T], F32R)
        raw = sb("raw", [P, NCH, CK, GC])
        w_high = sb("w_high", [P, SLOTS, CK, GC], F32R)
        w_low = sb("w_low", [P, SLOTS, CK, GC], F32R)
        mod_raw = sb("mod_raw", [P, SUBS, SK, STRIP_MAX])
        mod_acc = sb("mod_acc", [P, 2, 2, GC])
        stage = sb("stage", [P, 2, GT, T])
        gated = sb("gated", [P, GT, T + 2])
        ZC = T + P
        sig_rows = stage[:, :, :, :].rearrange("p a g t -> p (a g t)")
        soft = [sig_rows[:, i * ZC:(i + 1) * ZC] for i in range(2)]
        sp = [sig_rows[:, (2 + i) * ZC:(3 + i) * ZC] for i in range(3)]
        probs = sb("probs", [P, 3, ZC])
        vrow = sig_rows[:, 0:5 * P].rearrange("p (b n) -> p b n", b=5)
        ln_pair = probs[:, :, :].rearrange("p a z -> p (a z)")
        t_pair = ln_pair[:, 0:2 * T].rearrange("p (a t) -> p a t", a=2)
        q_pair = ln_pair[:, 2 * T:4 * T].rearrange("p (a t) -> p a t", a=2)
        vec = sb("vec", [P, V_ALL])
        mod = sb("mod", [P, DEPTH * MODT])
        cond = sb("cond", [P, 2, KT])
        coef = sb("coef", [P, 2 * DEPTH, 6, KT])
        coef0 = sb("coef0", [P, KT])
        ident = sb("ident", [P, P])
        mean_of = sb("mean_of", [P, P])
        ones = sb("ones", [P, 1])
        neg_ones = sb("neg_ones", [P, P])
        neg_tri = sb("neg_tri", [P, P])
        zeros = sb("zeros", [P, T])
        pivot_of = sb("pivot_of", [P, P])
        ln_tmp = sb("ln_tmp", [P, 6, T])
        var_t, root_t, new_t, piv_t, off_t, off2_t = (ln_tmp[:, i, :] for i in range(6))
        GATE1, SC1, A_, B_, RES_A, RES_B = range(6)

        bank = [ctx.enter_context(nc.psum_tensor(f"bank{i}", [P, 512], F32)) for i in range(8)]
        mod_ps = bank[4]
        piv_ps, off_ps, var_ps = bank[5], bank[6], bank[7]

        small_in = sem("small_in")
        x_in = sem("x_in")
        consts = sem("consts")
        raw_in = [sem(f"raw_in{j}") for j in range(NCH)]
        mod_in = [sem(f"mod_in{r}") for r in range(SUBS)]
        raw_used = sem("raw_used")
        high_done = sem("high_done")
        chunk_mult = sem("chunk_mult")
        banks_free = sem("banks_free")
        post_done = sem("post_done")
        hidden_high = sem("hidden_high")
        squared = sem("squared")
        mod_chain = sem("mod_chain")
        mod_sums = sem("mod_sums")
        mod_done = sem("mod_done")
        turned = sem("turned")
        turned_out = sem("turned_out")
        cond_act = sem("cond_act")
        cond_dve = sem("cond_dve")
        coefs = sem("coefs")
        h_act = sem("h_act")
        h_high_done = sem("h_high_done")
        h_done = sem("h_done")
        att_z, att_act, att_l = sem("att_z"), sem("att_act"), sem("att_l")
        att_sp, att_spm, att_cum = sem("att_sp"), sem("att_spm"), sem("att_cum")
        att_a, att_am, att_o = sem("att_a"), sem("att_am"), sem("att_o")
        att_hi, att_lo = sem("att_hi"), sem("att_lo")
        conv_step = sem("conv_step")
        conv_c = sem("conv_c")
        mod_comb = sem("mod_comb")
        ln_t = sem("ln_t")
        ln_base = sem("ln_base")
        ln_s = sem("ln_s")
        ln_piv = sem("ln_piv")
        ln_u = sem("ln_u")
        ln_sq = sem("ln_sq")
        ln_q = sem("ln_q")
        ln_off = sem("ln_off")
        ln_var = sem("ln_var")
        ln_rs = sem("ln_rs")
        ln_root = sem("ln_root")
        ln_y = sem("ln_y")
        ln_x = sem("ln_x")
        res_done = sem("res_done")
        y_init = sem("y_init")
        out_t = sem("out_t")
        out_c = sem("out_c")
        out_v = sem("out_v")
        out_dma = sem("out_dma")

        qkv_rows = attn_w_qkv[0].rearrange("(k p) n -> p k n", p=P)
        wo_rows = attn_w_o[0].rearrange("(k p) n -> p k n", p=P)
        cin_rows = conv_w_in[0].rearrange("(k p) n -> p k n", p=P)
        cout_rows = conv_w_out[0].rearrange("(k p) n -> p k n", p=P)
        w1_rows = [mlp_w1[i].rearrange("(k p) n -> p k n", p=P) for i in range(DEPTH)]
        w2_rows = [mlp_w2[i].rearrange("(k p) n -> p k n", p=P) for i in range(DEPTH)]
        mod_rows = [mod_w[i].rearrange("(k p) n -> p k n", p=P) for i in range(DEPTH)]

        block = ctx.enter_context(nc.Block())

        @block.sync
        def _(sp_):
            mod_units = mod_rows[0].rearrange("p k (u n) -> p k u n", n=D)
            for r in range(QUARTERS):
                for n in range(QC):
                    at = r * QC + n
                    slot = at % NCH
                    sp_.wait_ge(raw_used, at + 1)
                    if n < QM:
                        j, part = n // 2, 1 - n % 2
                        src = mod_units[:, CK * j:CK * (j + 1), part, r * GC:(r + 1) * GC]
                    else:
                        g, k = (n - QM) // 2, r * GT + CK * ((n - QM) % 2)
                        src = qkv_rows[:, k:k + CK, g * GC:(g + 1) * GC]
                    sp_.dma_start(raw[:, slot, :, :], src).then_inc(raw_in[slot], 16)

            def load_sub(strip, r):
                m, layer, tiles, t0 = strip
                sp_.wait_ge(mod_chain, m * KT + (MC0 - KT + SK * (r + 1)))
                sp_.dma_start(mod_raw[:, r, :, 0:tiles * P],
                              mod_rows[layer][:, SK * r:SK * (r + 1), ds(t0 * P, tiles * P)]
                              ).then_inc(mod_in[r], 16)

            def load_group(w, rows, k0, col, strip=None):
                for j in range(NCH):
                    sp_.wait_ge(raw_used, w * NCH + (PRE * NCH + j + 1))
                    sp_.dma_start(raw[:, j, :, :], rows[:, ds(k0 + CK * j, CK), ds(col, GC)]
                                  ).then_inc(raw_in[j], 16)
                    if strip and j >= NCH - SUBS:
                        load_sub(strip, j - (NCH - SUBS))

            def attn_strip(m):
                return (m + M_ATTN, 0, STRIP_ATTN, m * STRIP_ATTN + GATE_M * KT)

            with sp_.Fori(OPEN, 3 * NG) as g:
                load_group(g + W_QK, qkv_rows, 0, g * GC, attn_strip(g - OPEN))
            load_group(W_O, wo_rows, 0, 0)
            for m in range(3 * NG - OPEN, 3 * NG + 1):
                for r in range(SUBS):
                    load_sub(attn_strip(m), r)
            with sp_.Fori(1, NG) as g:
                load_group(g + W_O, wo_rows, 0, g * GC, attn_strip(g + 3 * NG))

            def load_mlp(layer):
                w0, m0 = W_MLP[layer], M_MLP[layer]
                per = 2 * NG if layer == 0 else NG
                with sp_.Fori(0, FC) as f:
                    with sp_.Fori(0, NG) as g:
                        load_group(f * (2 * NG) + g + w0, w1_rows[layer], 0, f * D + g * GC,
                                   (f * per + g + m0, layer, STRIP_W1, f * NG + g + GATE_F * KT))
                    with sp_.Fori(0, NG) as g:
                        load_group(f * (2 * NG) + g + (w0 + NG), w2_rows[layer], f * KT, g * GC,
                                   None if layer else
                                   (f * per + g + (m0 + NG), 1, STRIP_W2, (f * NG + g) * STRIP_W2))

            load_mlp(0)
            for n, part in enumerate((1, 2, 0)):
                with sp_.Fori(0, NG) as g:
                    load_group(g + (W_CIN + n * NG), cin_rows, 0, g * GC + part * D,
                               (g + (M_CONV + n * NG), 1, STRIP_CONV,
                                g * STRIP_CONV + (SHIFT_F * KT + n * NG * STRIP_CONV)))
            with sp_.Fori(0, NG) as g:
                load_group(g + W_COUT, cout_rows, 0, g * GC,
                           (g + (M_CONV + 3 * NG), 1, STRIP_CONV,
                            g * STRIP_CONV + (SHIFT_F * KT + 3 * NG * STRIP_CONV)))
            load_mlp(1)
            o_rows = out[0].rearrange("(t p) d -> p t d", p=P)
            for b in range(NG):
                for t in range(TT):
                    sp_.wait_ge((out_c, out_v)[t], b + 1)
                    sp_.dma_start(o_rows[:, t, b * GC:(b + 1) * GC], tok[:, t, b * GC:(b + 1) * GC]
                                  ).then_inc(out_dma, 16)
            sp_.wait_ge(out_dma, 16 * NG * TT)

        @block.gpsimd
        def _(pool):
            pool.memset(ident[:], 0.0).then_inc(consts, 1)
            pool.memset(neg_tri[:], -1.0).then_inc(consts, 1)
            pool.memset(neg_ones[:], -1.0).then_inc(consts, 1)
            pool.memset(mean_of[:], 1.0 / D).then_inc(consts, 1)
            pool.memset(ones[:], 1.0).then_inc(consts, 1)
            pool.memset(zeros[:], 0.0).then_inc(consts, 1)
            pool.memset(gated[:, :, 0:2], 0.0).then_inc(consts, 1)
            pool.memset(pivot_of[:], 1.0 / (D - GC)).then_inc(consts, 1)
            pool.wait_ge(consts, 8)
            pool.affine_select(out=ident[:], in_=ident[:], compare_op=ALU.not_equal, fill=1.0, base=0,
                               pattern=[[-1, P]], channel_multiplier=1).then_inc(consts, 1)
            pool.affine_select(out=neg_tri[:], in_=neg_tri[:], compare_op=ALU.is_ge, fill=0.0, base=0,
                               pattern=[[-1, P]], channel_multiplier=1).then_inc(consts, 1)

            def causal(t, done):
                v = t.rearrange("p (b q) -> p b q", b=3)[:, 0:3:2, :]
                pool.affine_select(out=v, in_=v, compare_op=ALU.is_gt, fill=0.0, base=0,
                                   pattern=[[0, 2], [1, P]], channel_multiplier=-1).then_inc(done, 1)

            for s in range(HEADS + 2):
                if s < HEADS:
                    pool.wait_ge(att_sp, s + 1)
                    causal(sp[s % 3], att_spm)
                if s >= 2:
                    pool.wait_ge(att_a, s - 1)
                    causal(probs[:, (s - 2) % 3, :], att_am)

            n_coef = [0]

            def step(ins):
                n_coef[0] += 1
                ins.then_inc(coefs, 1)
                pool.wait_ge(coefs, n_coef[0])

            def gate_coefficient(n):
                layer, half = n // 2, n % 2
                gate = layer * MODT + (GATE_F if half else GATE_M) * KT
                step(pool.tensor_scalar(coef[:, n, GATE1], mod[:, gate:gate + KT], 1.0, 1.0, ALU.add, ALU.mult))

            def sum_squares(n):
                for b in range(NG - 1):
                    pool.wait_ge(ln_sq, 7 * n + b + 1)
                    s = stage[:, b % 2]
                    for a in range(2):
                        if b == 0 and a == 0:
                            continue
                        first = b == 0
                        if not first:
                            pool.wait_ge(ln_q, 5 * n + 2 * b + a - 1)
                        pool.tensor_tensor(q_pair, s[:, 0:2] if first else q_pair, s[:, 2 * a:2 * a + 2],
                                           ALU.add).then_inc(ln_q, 1)

            def coefficients(n):
                half = n % 2
                g = vec[:, V_LNG + n * KT:V_LNG + (n + 1) * KT]
                b = vec[:, V_LNB + n * KT:V_LNB + (n + 1) * KT]
                k = coef[:, n]
                nl = (n + 1) // 2
                sh = nl * MODT + (SHIFT_M if half else SHIFT_F) * KT
                sc = sh + KT
                step(pool.tensor_scalar(k[:, SC1], mod[:, sc:sc + KT], 1.0, 1.0, ALU.add, ALU.mult))
                step(pool.tensor_tensor(k[:, A_], k[:, SC1], g, ALU.mult))
                step(pool.tensor_tensor(k[:, B_], k[:, SC1], b, ALU.mult))
                step(pool.tensor_tensor(k[:, B_], k[:, B_], mod[:, sh:sh + KT], ALU.add))
                step(pool.tensor_scalar(k[:, RES_A], g, ALPHA, 0.0, ALU.mult, ALU.add))
                step(pool.tensor_scalar(k[:, RES_B], b, ALPHA, 0.0, ALU.mult, ALU.add))

            def residual(n):
                for m in range(KT):
                    pool.wait_ge(ln_x, n * KT + m + 1)
                    pool.tensor_scalar(res[:, m, :], y[:, m, :], coef[:, n, RES_A, m:m + 1],
                                       coef[:, n, RES_B, m:m + 1], ALU.mult, ALU.add).then_inc(res_done, 1)
                    if n % 2 == 0:
                        b2 = V_B2 + (n // 2) * KT + m
                        pool.wait_ge(h_act, (n + 1) * KT + m + 1)
                        pool.wait_ge(res_done, n * KT + m + 1)
                        pool.tensor_scalar(y[:, m, :], zeros[:], vec[:, b2:b2 + 1], 1.0, ALU.add, ALU.mult
                                           ).then_inc(y_init, 1)

            gate_need = [KT // STRIP_ATTN + 1, M_CONV - NG, M_CONV, M_MLP[1] + NG * FC]
            need = [M_MLP[0], M_CONV, M_MLP[1]]
            for n in range(2 * DEPTH):
                pool.wait_ge(mod_done, MD0 + gate_need[n])
                gate_coefficient(n)
                sum_squares(n)
                if n < 2 * DEPTH - 1:
                    pool.wait_ge(mod_done, MD0 + need[n])
                    coefficients(n)
                    residual(n)

        GATE_DONE = [7 * n + 1 for n in range(2 * DEPTH)]
        COEF_DONE = [7 * n + 7 for n in range(2 * DEPTH - 1)]
        BLOCKS = [(0, 1), (1, 2), (2, 4)] + [(GT * b, GT * (b + 1)) for b in range(1, NG)]

        def stage_tiles(m0, m1):
            return stage[:, (m0 // GT) % 2, m0 % GT:m0 % GT + m1 - m0, :]

        @block.scalar
        def _(act):
            batches = [
                [c.rearrange("b (k p) -> (b k) p", p=P), mod_b[0].rearrange("(k p) -> k p", p=P)],
                [mod_b[1].rearrange("(k p) -> k p", p=P)],
                [ln_g.rearrange("i j (k p) -> (i j k) p", p=P), ln_b.rearrange("i j (k p) -> (i j k) p", p=P)],
                [conv_w.rearrange("i w (k p) -> (i w k) p", p=P), conv_b.rearrange("i (k p) -> (i k) p", p=P),
                 mlp_b2.rearrange("i (k p) -> (i k) p", p=P)],
                [mlp_b1.rearrange("i (k p) -> (i k) p", p=P)],
            ]
            for b, parts in enumerate(batches):
                row = 0
                for part in parts:
                    n = part.shape[0]
                    act.dma_start(vrow[row:row + n, b, :], part).then_inc(small_in, 16)
                    row += n
            act.dma_start(tok[:, :, :], x[0].rearrange("(t p) d -> p t d", p=P)).then_inc(x_in, 16)
            act.preload_act_table_set("natural_log_exp_and_others")
            act.nop().then_inc(banks_free, CREDIT_BANKS)
            act.wait_ge(turned, 5)
            act.activation(vec[:, 0:V_CW], bank[7][:, 0:V_CW], ACT.Copy).then_inc(turned_out, 1)
            act.activation(vec[:, V_CW:V_ALL], bank[6][:, 0:V_ALL - V_CW], ACT.Copy).then_inc(turned_out, 1)
            act.wait_ge(turned_out, 1)
            act.activation(cond[:, 0, :], vec[:, V_C:V_C + KT], ACT.Exp, scale=-1.0).then_inc(cond_act, 1)
            for b in range(TT * NG):
                t, g = b // NG, b % NG
                act.wait_ge(turned, 5 + b + 1)
                act.activation(res[:, GT * g:GT * (g + 1), t * P:(t + 1) * P],
                               bank[b % 4][:, :].rearrange("p (k t) -> p k t", k=GT), ACT.Copy,
                               scale=ALPHA).then_inc(turned_out, 1)

            def high(w, j):
                act.wait_ge(raw_in[j], (w + PRE) * 16 + 16)
                act.wait_ge(chunk_mult, w * NCH + (j + 1))
                act.activation(w_high[:, j % SLOTS], raw[:, j], ACT.Copy).then_inc(high_done, 1)

            def highs(w):
                for j in range(SLOTS, NCH):
                    high(w, j)
                for j in range(SLOTS):
                    high(w + 1, j)
                act.wait_ge(chunk_mult, w * NCH + (CREDIT_SPLIT + NCH))

            def make_h(n):
                act.wait_ge(coefs, COEF_DONE[n - 1])
                for m0, m1 in BLOCKS:
                    act.wait_ge(ln_x, (n - 1) * KT + m1)
                    if m0 >= 2 * GT:
                        act.wait_ge(h_done, n * KT + m1 - 2 * GT)
                    else:
                        act.wait_ge(ln_var, n)
                    for m in range(m0, m1):
                        ins = act.activation(stage_tiles(m, m + 1)[:, 0, :], y[:, m, :], ACT.Identity,
                                             scale=coef[:, n - 1, A_, m:m + 1], bias=coef[:, n - 1, B_, m:m + 1])
                        ins.then_inc(h_act, 1)
                    act.wait_ge(h_act, n * KT + m1)
                    act.activation(h_high[:, m0:m1, :], stage_tiles(m0, m1), ACT.Copy).then_inc(h_high_done, m1 - m0)

            act.wait_ge(turned_out, 2 + TT * NG)
            with act.Fori(0, QUARTERS // 2) as i:
                for q in range(2):
                    for n in range(QW):
                        at = q * QC + QM + n
                        act.wait_ge(raw_in[at % NCH], i * (16 * 2 * QC // NCH) + 16 * (at // NCH + 1))
                        act.wait_ge(chunk_mult, i * (2 * QW) + (q * QW + n + 1))
                        act.activation(w_high[:, n % SLOTS], raw[:, at % NCH], ACT.Copy).then_inc(high_done, 1)
                    act.wait_ge(cond_dve, i * 2 + (q + 4))
                    for m in range(GT):
                        t = i * (2 * GT) + (q * GT + m)
                        act.activation(stage[:, q, m, :], res[:, ds(t, 1), :].rearrange("p k t -> p (k t)"),
                                       ACT.Identity, scale=coef0[:, ds(t, 1)], bias=mod[:, ds(t, 1)]
                                       ).then_inc(h_act, 1)
                    act.wait_ge(h_act, i * (2 * GT) + (q + 1) * GT)
                    act.activation(h_high[:, ds(i * (2 * GT) + q * GT, GT), :], stage[:, q], ACT.Copy
                                   ).then_inc(h_high_done, GT)
            for j in range(SLOTS):
                high(OPEN, j)
            act.wait_ge(chunk_mult, OPEN * NCH + CREDIT_SPLIT)

            def empty(w, par, dst, scale=1.0, inc=banks_free):
                act.activation(dst(0), bank[2 * par][:, :], ACT.Copy, scale=scale)
                act.activation(dst(1), bank[2 * par + 1][:, :], ACT.Copy, scale=scale).then_inc(banks_free, 1)

            def to_tiles(t, g):
                return lambda b: t[:, ds(g * GT + 2 * b, 2), :].rearrange("p k t -> p (k t)")

            for g in range(OPEN):
                empty(None, g, to_tiles(q_t, g), ZSCALE)
            for g in range(OPEN, NG):
                highs(W_QK + g)
                empty(None, g % 2, to_tiles(q_t, g), ZSCALE)
            with act.Fori(0, NG // 2) as i:
                for par in range(2):
                    highs(i * 2 + (W_QK + NG + par))
                    empty(None, par, to_tiles(k_t, i * 2 + par))
            with act.Fori(0, NG // 2) as i:
                for par in range(2):
                    highs(i * 2 + (W_V + par))
                    empty(None, par, lambda b: v_tok[:, b, ds((i * 2 + par) * GC, GC)])

            for s in range(HEADS + 2):
                if s < HEADS:
                    e = soft[s % 2]
                    act.wait_ge(att_z, s + 1)
                    if s >= 2:
                        act.wait_ge(att_sp, s - 1)
                    act.activation(e, bank[s % 4][:, 0:ZC], ACT.Abs).then_inc(att_act, 1)
                    act.wait_ge(att_act, 2 * s + 1)
                    act.activation(e, e, ACT.Exp, scale=-1.0).then_inc(att_act, 1)
                    act.wait_ge(att_act, 2 * s + 2)
                    act.activation(e, e, ACT.Ln, bias=1.0).then_inc(att_l, 1)
                if s >= 2:
                    a = s - 2
                    act.wait_ge(att_cum, a + 1)
                    if a >= 3:
                        act.wait_ge(att_o, a - 2)
                    act.activation(probs[:, a % 3, :], bank[a % 4][:, 0:ZC], ACT.Exp).then_inc(att_a, 1)

            def tail(n, w0):
                for g in range(NG):
                    if g < NG - 1:
                        highs(w0 + g)
                        act.wait_ge(ln_t, n * KT + GT * (g + 1))
                        act.nop().then_inc(banks_free, 1)
                        continue
                    for j in range(SLOTS, NCH):
                        high(w0 + g, j)
                    act.wait_ge(ln_piv, 2 * n + 1)
                    act.activation(piv_t, piv_ps[:, 0:T], ACT.Copy).then_inc(ln_piv, 1)
                    for b in range(NG - 1):
                        act.wait_ge(ln_u, (NG * n) + b + 1)
                        if b >= 2:
                            act.wait_ge(ln_q, 5 * n + 1)
                        act.activation(stage[:, b % 2], y[:, GT * b:GT * (b + 1), :], ACT.Square
                                       ).then_inc(ln_sq, 1)
                    if n < 2 * DEPTH - 1:
                        for j in range(SLOTS):
                            high(w0 + g + 1, j)
                    act.wait_ge(ln_q, 5 * n + 3)
                    for m in range(KT - GT, KT):
                        act.wait_ge(ln_t, n * KT + m + 1)
                        act.activation(stage[:, 1, m % GT, :], y[:, m, :], ACT.Square).then_inc(ln_sq, 1)
                    act.nop().then_inc(banks_free, 1)
                act.wait_ge(ln_off, 3 * n + 1)
                act.activation(off2_t, off_ps[:, 0:T], ACT.Square).then_inc(ln_off, 1)
                act.activation(off_t, off_ps[:, 0:T], ACT.Copy).then_inc(ln_off, 1)
                act.wait_ge(ln_rs, 4 * n + 1)
                act.activation(root_t, var_t, ACT.Ln).then_inc(ln_root, 1)
                act.wait_ge(ln_root, 2 * n + 1)
                act.activation(root_t, root_t, ACT.Exp, scale=-0.5).then_inc(ln_root, 1)
                if n < 2 * DEPTH - 1:
                    make_h(n + 1)

            def hidden_group(layer, f, g, par):
                w = f * (2 * NG) + g + W_MLP[layer]
                highs(w)
                act.wait_ge(post_done, f * (2 * NG) + g + (S_MLP[layer] + 1))
                b1 = V_B1 + layer * (FF // P)
                for m in range(GT):
                    ins = act.activation(stage[:, par, m, :], bank[2 * par + m // 2][:, T * (m % 2):T * (m % 2 + 1)],
                                         ACT.Relu, bias=vec[:, ds(f * KT + g * GT + (b1 + m), 1)])
                ins.then_inc(banks_free, 1)
                act.wait_ge(banks_free, w + (CREDIT_BANKS + 1))
                act.activation(stage[:, par], stage[:, par], ACT.Square).then_inc(squared, 1)
                act.wait_ge(squared, f * NG + g + (layer * NG * FC + 1))
                act.activation(hid_high[:, ds(g * GT, GT), :], stage[:, par], ACT.Copy).then_inc(hidden_high, 1)

            def down_group(layer, f, g, par):
                w = f * (2 * NG) + g + (W_MLP[layer] + NG)
                highs(w)
                act.wait_ge(post_done, f * (2 * NG) + g + (S_MLP[layer] + NG + 1))
                empty(None, par, lambda b: stage[:, par, 2 * b:2 * b + 2, :].rearrange("p k t -> p (k t)"))

            def mlp_up(layer, f):
                with act.Fori(0, NG // 2) as i:
                    for par in range(2):
                        hidden_group(layer, f, i * 2 + par, par)

            def mlp(layer):
                with act.Fori(0, FC - 1) as f:
                    mlp_up(layer, f)
                    with act.Fori(0, NG // 2) as i:
                        for par in range(2):
                            down_group(layer, f, i * 2 + par, par)
                mlp_up(layer, FC - 1)
                tail(2 * layer + 1, W_MLP[layer] + 2 * NG * FC - NG)

            tail(0, W_O)
            mlp(0)
            act.wait_ge(res_done, 2 * KT)
            with act.Fori(0, NG // 2) as i:
                for par in range(2):
                    highs(i * 2 + (W_CIN + par))
                    empty(None, par, to_tiles(y, i * 2 + par))
            with act.Fori(0, NG) as i:
                for par in range(2):
                    highs(i * 2 + (W_CIN + NG + par))
                    act.wait_ge(post_done, i * 2 + (S_CONV + par + 1))
                    empty(None, par, lambda b: stage[:, par, 2 * b:2 * b + 2, :].rearrange("p k t -> p (k t)"))
            tail(2, W_COUT)
            mlp(1)
            n = 2 * DEPTH - 1

            def rows_out(b):
                act.wait_ge(out_t, TT * b + 1)
                act.activation(tok[:, 0, b * GC:(b + 1) * GC], bank[(TT * b) % 4][:, :], ACT.Copy
                               ).then_inc(out_c, 1)

            for b in range(NG):
                if b >= 2:
                    act.wait_ge(out_t, TT * (b - 1))
                else:
                    act.wait_ge(ln_var, n + 1)
                for m in range(GT * b, GT * (b + 1)):
                    act.wait_ge(ln_x, n * KT + m + 1)
                    act.activation(stage[:, b % 2, m % GT, :], y[:, m, :], ACT.Identity,
                                   scale=vec[:, V_LNG + n * KT + m:V_LNG + n * KT + m + 1],
                                   bias=vec[:, V_LNB + n * KT + m:V_LNB + n * KT + m + 1]
                                   ).then_inc(h_act, 1)
                if b:
                    rows_out(b - 1)
            rows_out(NG - 1)

        @block.vector
        def _(dve):
            dve.nop().then_inc(raw_used, CREDIT_RAW)
            dve.nop().then_inc(post_done, CREDIT_STAGE)
            dve.wait_ge(cond_act, 1)
            dve.tensor_scalar(cond[:, 0, :], cond[:, 0, :], 1.0, None, ALU.add).then_inc(cond_dve, 1)
            dve.wait_ge(cond_dve, 1)
            dve.reciprocal(cond[:, 0, :], cond[:, 0, :]).then_inc(cond_dve, 1)
            dve.wait_ge(cond_dve, 2)
            dve.wait_ge(turned_out, 2)
            dve.tensor_tensor(cond[:, 1, :], cond[:, 0, :], vec[:, V_C:V_C + KT], ALU.mult).then_inc(cond_dve, 1)
            dve.wait_ge(cond_dve, 3)

            def add_rows(m, k, rows, cols):
                acc = mod_acc[:, k % 2, 0, 0:cols]
                if k < 2:
                    dve.tensor_scalar(acc, rows, cond[:, 1, k:k + 1], None, ALU.mult).then_inc(mod_chain, 1)
                else:
                    dve.wait_ge(mod_chain, m * KT + (MC0 + k - 1))
                    dve.scalar_tensor_tensor(out=acc, in0=rows, scalar=cond[:, 1, k:k + 1], in1=acc,
                                             op0=ALU.mult, op1=ALU.add).then_inc(mod_chain, 1)

            def add_sub(m, r, tiles):
                dve.wait_ge(mod_in[r], m * 16 + 16)
                for k in range(SK):
                    add_rows(m, SK * r + k, mod_raw[:, r, k, 0:tiles * P], tiles * P)

            def combine(m, tiles):
                dve.wait_ge(mod_chain, m * KT + (MC0 + KT))
                dve.tensor_tensor(mod_acc[:, 0, 0, 0:tiles * P], mod_acc[:, 0, 0, 0:tiles * P],
                                  mod_acc[:, 1, 0, 0:tiles * P], ALU.add).then_inc(mod_comb, 1)

            def write_mod(m, tile, tiles):
                dve.wait_ge(mod_sums, m + (QUARTERS + 1))
                dve.tensor_tensor(mod[:, ds(tile, tiles)], mod_ps[:, 0:tiles], vec[:, ds(tile + V_MODB, tiles)],
                                  ALU.add).then_inc(mod_done, 1)

            with dve.Fori(0, QUARTERS // 2) as i:
                for q in range(2):
                    r = i * 2 + q
                    for n in range(QM):
                        at = q * QC + n
                        j, part = n // 2, n % 2
                        dve.wait_ge(raw_in[at % NCH], i * (16 * 2 * QC // NCH) + 16 * (at // NCH + 1))
                        for k in range(CK):
                            acc = mod_acc[:, k, part, :]
                            rows = raw[:, at % NCH, k, :]
                            c1 = cond[:, 1, CK * j + k:CK * j + k + 1]
                            if j == 0:
                                ins = dve.tensor_scalar(acc, rows, c1, None, ALU.mult)
                            else:
                                if k == 0:
                                    dve.wait_ge(mod_chain, i * (2 * QM) + (q * QM + n - 1))
                                else:
                                    dve.wait_ge(raw_used, i * (2 * QC) + (CREDIT_RAW + at - 1))
                                ins = dve.scalar_tensor_tensor(out=acc, in0=rows, scalar=c1, in1=acc,
                                                               op0=ALU.mult, op1=ALU.add)
                            ins.then_inc(mod_chain if k == 0 else raw_used, 1)
                    dve.wait_ge(mod_chain, i * (2 * QM) + (q + 1) * QM)
                    dve.wait_ge(raw_used, i * (2 * QC) + (CREDIT_RAW + q * QC + QM))
                    dve.tensor_tensor(mod_acc[:, 0], mod_acc[:, 0], mod_acc[:, 1], ALU.add).then_inc(mod_comb, 1)
                    for n in range(QW):
                        at = q * QC + QM + n
                        dve.wait_ge(high_done, i * (2 * QW) + (q * QW + n + 1))
                        dve.tensor_tensor(w_low[:, n % SLOTS], raw[:, at % NCH], w_high[:, n % SLOTS].bitcast(F32),
                                          ALU.subtract).then_inc(raw_used, 1)
                    dve.wait_ge(mod_sums, r + 1)
                    for part, unit in ((0, SCALE_M), (1, SHIFT_M)):
                        dve.tensor_tensor(mod[:, ds(r * GT + unit * KT, GT)], mod_ps[:, GT * part:GT * (part + 1)],
                                          vec[:, ds(r * GT + (V_MODB + unit * KT), GT)], ALU.add
                                          ).then_inc(mod_done, 1)
                    dve.wait_ge(mod_done, i * 4 + 2 * (q + 1))
                    dve.tensor_scalar(coef0[:, ds(r * GT, GT)], mod[:, ds(r * GT + SCALE_M * KT, GT)], 1.0,
                                      1.0 / ALPHA, ALU.add, ALU.mult).then_inc(cond_dve, 1)
                    dve.wait_ge(h_high_done, i * (2 * GT) + (q + 1) * GT)
                    hs = ds(i * (2 * GT) + q * GT, GT)
                    dve.tensor_tensor(h_low[:, hs, :], stage[:, q], h_high[:, hs, :].bitcast(F32), ALU.subtract
                                      ).then_inc(h_done, GT)

            def low(w, j):
                dve.wait_ge(high_done, w * NCH + (j + 1))
                dve.tensor_tensor(w_low[:, j % SLOTS], raw[:, j], w_high[:, j % SLOTS].bitcast(F32),
                                  ALU.subtract).then_inc(raw_used, 1)

            def lows(w, strip=None, between=None, last=False):
                for j in range(SLOTS, NCH):
                    low(w, j)
                    if strip:
                        add_sub(strip[0], j - SLOTS, strip[1])
                if between:
                    between()
                for j in range(0 if last else SLOTS):
                    low(w + 1, j)
                    if strip and j == 0:
                        combine(*strip)

            def low_h(n, m0, m1):
                dve.wait_ge(h_high_done, n * KT + m1)
                dve.tensor_tensor(h_low[:, m0:m1, :], stage_tiles(m0, m1), h_high[:, m0:m1, :].bitcast(F32),
                                  ALU.subtract).then_inc(h_done, m1 - m0)

            for j in range(SLOTS):
                low(OPEN, j)

            with dve.Fori(0, 3 * NG - OPEN) as g:
                lows(g + (W_QK + OPEN), (g + M_ATTN, STRIP_ATTN))
                write_mod(g + M_ATTN, g * STRIP_ATTN + GATE_M * KT, STRIP_ATTN)

            for s in range(HEADS + 3):
                if s < HEADS:
                    dve.wait_ge(att_l, s + 1)
                    if s >= 3:
                        dve.wait_ge(att_cum, s - 2)
                    dve.scalar_tensor_tensor(out=sp[s % 3], in0=bank[s % 4][:, 0:ZC], scalar=0.0,
                                             in1=soft[s % 2], op0=ALU.max, op1=ALU.add).then_inc(att_sp, 1)
                if s >= 3:
                    o = s - 3
                    dve.wait_ge(att_o, o + 1)
                    dve.tensor_copy(h_high[:, o, :], bank[6 + o % 2][:, 0:T]).then_inc(att_hi, 1)
                    dve.wait_ge(att_hi, o + 1)
                    dve.tensor_tensor(h_low[:, o, :], bank[6 + o % 2][:, 0:T], h_high[:, o, :].bitcast(F32),
                                      ALU.subtract).then_inc(att_lo, 1)
                if s in (2 * SUBS, 4 * SUBS):
                    m = 3 * NG - OPEN + s // (2 * SUBS) - 1
                    write_mod(m, m * STRIP_ATTN + GATE_M * KT, STRIP_ATTN)
                if s % 2 == 0 and s < HEADS:
                    m = 3 * NG - OPEN + s // (2 * SUBS)
                    add_sub(m, (s // 2) % SUBS, STRIP_ATTN)
                    if (s // 2) % SUBS == SUBS - 1:
                        combine(m, STRIP_ATTN)

            def layer_norm(n):
                dve.wait_ge(ln_off, 3 * n + 3)
                dve.wait_ge(ln_var, n + 1)
                dve.scalar_tensor_tensor(out=var_t, in0=var_ps[:, 0:T], scalar=EPS, in1=off2_t, op0=ALU.add,
                                         op1=ALU.subtract).then_inc(ln_rs, 1)
                dve.wait_ge(ln_root, 2 * n + 2)
                dve.tensor_tensor(new_t, root_t, root_t, ALU.mult).then_inc(ln_rs, 1)
                dve.wait_ge(ln_rs, 4 * n + 2)
                dve.scalar_tensor_tensor(out=new_t, in0=new_t, scalar=-0.5, in1=var_t, op0=ALU.mult,
                                         op1=ALU.mult).then_inc(ln_rs, 1)
                dve.wait_ge(ln_rs, 4 * n + 3)
                dve.scalar_tensor_tensor(out=root_t, in0=new_t, scalar=1.5, in1=root_t, op0=ALU.add,
                                         op1=ALU.mult).then_inc(ln_rs, 1)
                dve.wait_ge(ln_rs, 4 * n + 4)

                def normalise(m0, m1):
                    k = m1 - m0
                    yt = y[:, m0:m1, :]
                    off, root = (t.unsqueeze(1).to_broadcast([P, k, T]) for t in (off_t, root_t))
                    dve.tensor_tensor(yt, yt, off, ALU.subtract).then_inc(ln_y, 1)
                    dve.wait_ge(ln_y, len(BLOCKS) * n + BLOCKS.index((m0, m1)) + 1)
                    dve.tensor_tensor(yt, yt, root, ALU.mult).then_inc(ln_x, k)

                more = n < 2 * DEPTH - 1
                for b in range(len(BLOCKS) + 1):
                    if b < len(BLOCKS):
                        normalise(*BLOCKS[b])
                    if more and b >= 1:
                        low_h(n + 1, *BLOCKS[b - 1])

            def tail(n, w0, strips):
                mlp = n % 2 == 1
                base = y if mlp else res
                dve.wait_ge(coefs, GATE_DONE[n])
                if n:
                    dve.wait_ge(res_done, n * KT)
                if mlp:
                    dve.wait_ge(post_done, CREDIT_STAGE + S_MLP[n // 2] + 2 * NG * FC - NG)
                piv = piv_t.unsqueeze(1).to_broadcast([P, GT, T])
                for g in range(NG):
                    last = g == NG - 1
                    if mlp:
                        for m in range(GT * g, GT * (g + 1)):
                            dve.scalar_tensor_tensor(out=y[:, m, :], in0=y[:, m, :],
                                                     scalar=coef[:, n, GATE1, m:m + 1], in1=res[:, m, :],
                                                     op0=ALU.mult, op1=ALU.add).then_inc(ln_base, 1)

                    def pivot():
                        dve.wait_ge(ln_piv, 2 * n + 2)
                        for b in range(NG):
                            ts = slice(GT * b, GT * (b + 1))
                            src = y if b < NG - 1 else base
                            if b == NG - 1 and mlp:
                                dve.wait_ge(ln_base, (n // 2 + 1) * KT)
                            dve.tensor_tensor(y[:, ts, :], src[:, ts, :], piv, ALU.subtract).then_inc(ln_u, 1)

                    lows(w0 + g, strips and (strips[0] + g, strips[1]), pivot if last else None,
                         last and n == 2 * DEPTH - 1)
                    dve.wait_ge(chunk_mult, (w0 + g) * NCH + (CREDIT_SPLIT + NCH))
                    if last:
                        dve.wait_ge(ln_u, NG * (n + 1))
                    elif mlp:
                        dve.wait_ge(ln_base, (n // 2) * KT + GT * (g + 1))
                    for m in range(GT * g, GT * (g + 1)):
                        b = bank[2 * (g % 2) + (m % GT) // 2]
                        dve.scalar_tensor_tensor(out=y[:, m, :], in0=b[:, T * (m % 2):T * (m % 2 + 1)],
                                                 scalar=coef[:, n, GATE1, m:m + 1],
                                                 in1=(y if last else base)[:, m, :], op0=ALU.mult, op1=ALU.add
                                                 ).then_inc(ln_t, 1)
                    if not last:
                        dve.wait_ge(ln_t, n * KT + GT * (g + 1))
                        for a in range(2):
                            if g == 0 and a == 0:
                                continue
                            if g:
                                dve.wait_ge(ln_s, 5 * n + 2 * g + a - 1)
                            dve.tensor_tensor(t_pair, y[:, 0:2, :] if g == 0 else t_pair,
                                              y[:, GT * g + 2 * a:GT * g + 2 * a + 2, :], ALU.add
                                              ).then_inc(ln_s, 1)
                    if strips:
                        write_mod(strips[0] + g, strips[2] + g * strips[1], strips[1])
                layer_norm(n)

            tail(0, W_O, (M_ATTN + 3 * NG, STRIP_ATTN, GATE_M * KT + 3 * NG * STRIP_ATTN))

            def hidden_group(layer, f, g, par):
                m = f * (2 * NG if layer == 0 else NG) + g + M_MLP[layer]
                lows(f * (2 * NG) + g + W_MLP[layer], (m, STRIP_W1))
                dve.wait_ge(hidden_high, f * NG + g + (layer * NG * FC + 1))
                dve.tensor_tensor(hid_low[:, ds(g * GT, GT), :], stage[:, par],
                                  hid_high[:, ds(g * GT, GT), :].bitcast(F32), ALU.subtract).then_inc(post_done, 1)
                write_mod(m, f * NG + g + (layer * MODT + GATE_F * KT), STRIP_W1)

            def down_group(layer, f, g, par):
                w = f * (2 * NG) + g + (W_MLP[layer] + NG)
                m = f * (2 * NG) + g + (M_MLP[layer] + NG)
                lows(w, (m, STRIP_W2) if layer == 0 else None)
                dve.wait_ge(banks_free, w + (CREDIT_BANKS + 1))
                dve.wait_ge(post_done, f * (2 * NG) + g + (CREDIT_STAGE + S_MLP[layer] + NG))
                yt = y[:, ds(g * GT, GT), :]
                dve.tensor_tensor(yt, yt, stage[:, par], ALU.add).then_inc(post_done, 1)
                if layer == 0:
                    write_mod(m, (f * NG + g) * STRIP_W2 + MODT, STRIP_W2)

            def mlp(layer):
                def up(f):
                    with dve.Fori(0, NG // 2) as i:
                        for par in range(2):
                            hidden_group(layer, f, i * 2 + par, par)

                dve.wait_ge(y_init, (layer + 1) * KT)
                with dve.Fori(0, FC - 1) as f:
                    up(f)
                    with dve.Fori(0, NG // 2) as i:
                        for par in range(2):
                            down_group(layer, f, i * 2 + par, par)
                up(FC - 1)
                tail(2 * layer + 1, W_MLP[layer] + 2 * NG * FC - NG,
                     None if layer else (M_CONV - NG, STRIP_W2, MODT + (FC - 1) * NG * STRIP_W2))

            mlp(0)

            with dve.Fori(0, NG) as g:
                lows(g + W_CIN, (g + M_CONV, STRIP_CONV))
                write_mod(g + (M_CONV), g * STRIP_CONV + (MODT + SHIFT_F * KT), STRIP_CONV)
            with dve.Fori(0, NG // 2) as i:
                for par in range(2):
                    g = i * 2 + par
                    w = g + (W_CIN + NG)
                    lows(w, (g + (M_CONV + NG), STRIP_CONV))
                    dve.wait_ge(banks_free, w + (CREDIT_BANKS + 1))
                    dve.wait_ge(post_done, g + (CREDIT_STAGE + S_CONV))
                    dve.tensor_tensor(gated[:, :, 2:T + 2], stage[:, par], y[:, ds(g * GT, GT), :], ALU.mult
                                      ).then_inc(conv_step, 1)
                    steps = 1 + 2 * GT
                    for tap in (2, 1, 0):
                        for m in range(GT):
                            yt = y[:, ds(g * GT + m, 1), :].rearrange("p k t -> p (k t)")
                            cw = vec[:, ds(g * GT + (V_CW + tap * KT + m), 1)]
                            src = gated[:, m, tap:tap + T]
                            dve.wait_ge(conv_step, g * steps + (1 if tap == 2 else 1 + (1 - tap) * GT + m + 1))
                            if tap == 2:
                                dve.tensor_scalar(yt, src, cw, vec[:, ds(g * GT + (V_CB + m), 1)], ALU.mult,
                                                  ALU.add).then_inc(conv_step, 1)
                            else:
                                ins = dve.scalar_tensor_tensor(out=yt, in0=src, scalar=cw, in1=yt, op0=ALU.mult,
                                                               op1=ALU.add)
                                if tap == 1:
                                    ins.then_inc(conv_step, 1)
                    ins.then_inc(post_done, 1)
                    write_mod(g + (M_CONV + NG),
                              g * STRIP_CONV + (MODT + SHIFT_F * KT + NG * STRIP_CONV), STRIP_CONV)
            with dve.Fori(0, NG // 2) as i:
                for par in range(2):
                    g = i * 2 + par
                    w = g + (W_CIN + 2 * NG)
                    lows(w, (g + (M_CONV + 2 * NG), STRIP_CONV))
                    dve.wait_ge(banks_free, w + (CREDIT_BANKS + 1))
                    dve.wait_ge(post_done, g + (CREDIT_STAGE + S_CONV + NG))
                    st, hg = stage[:, par], hid_high[:, ds(g * GT, GT), :]
                    dve.tensor_tensor(st, st, y[:, ds(g * GT, GT), :], ALU.mult).then_inc(conv_c, 1)
                    dve.wait_ge(conv_c, g * 2 + 1)
                    dve.tensor_copy(hg, st).then_inc(conv_c, 1)
                    dve.wait_ge(conv_c, g * 2 + 2)
                    dve.tensor_tensor(hid_low[:, ds(g * GT, GT), :], st, hg.bitcast(F32), ALU.subtract
                                      ).then_inc(post_done, 1)
                    write_mod(g + (M_CONV + 2 * NG),
                              g * STRIP_CONV + (MODT + SHIFT_F * KT + 2 * NG * STRIP_CONV), STRIP_CONV)
            tail(2, W_COUT, (M_CONV + 3 * NG, STRIP_CONV, MODT + SHIFT_F * KT + 3 * NG * STRIP_CONV))
            mlp(1)
            for b in range(NG):
                dve.wait_ge(out_t, TT * (b + 1))
                dve.tensor_copy(tok[:, 1, b * GC:(b + 1) * GC], bank[(TT * b + 1) % 4][:, :]).then_inc(out_v, 1)

        @block.tensor
        def _(pe):
            pe.nop().then_inc(chunk_mult, CREDIT_SPLIT)
            pe.wait_ge(consts, 9)
            pe.wait_ge(small_in, 16 * 9)
            rows = [KT + MODT, MODT, 4 * DEPTH * KT, 4 * KT + DEPTH * KT, DEPTH * FF // P]
            at = [0, KT + MODT, V_LNG, 0, V_B1 - V_CW]
            for b, n in enumerate(rows):
                dst = bank[7 if b < 3 else 6]
                pe.transpose(dst[:, at[b]:at[b] + n], vrow[0:n, b, :], ident[0:n, 0:n]).then_inc(turned, 1)
            pe.wait_ge(x_in, 16)
            for b in range(TT * NG):
                t, g = b // NG, b % NG
                if b >= 4:
                    pe.wait_ge(turned_out, 2 + b - 3)
                for m in range(GT):
                    ins = pe.transpose(bank[b % 4][:, m * P:(m + 1) * P],
                                       tok[:, t, (GT * g + m) * P:(GT * g + m + 1) * P], ident[:])
                ins.then_inc(turned, 1)

            def tile_row(par, k, wh, wl, high, low, tokens=False):
                for m in range(TT if tokens else GT):
                    s = slice(m * P, (m + 1) * P)
                    if tokens:
                        dst = bank[2 * par + m][:, :]
                        pairs = [(high[:, k, s], wh), (high[:, k, s], wl), (low[:, k, s], wh)]
                        first = k == 0
                    else:
                        dst = bank[2 * par + m // 2][:, T * (m % 2):T * (m % 2 + 1)]
                        pairs = [(wh[:, s], high[:, k, :]), (wh[:, s], low[:, k, :]), (wl[:, s], high[:, k, :])]
                        first = k == 0 and m % 2 == 0
                    for n, (a, b) in enumerate(pairs):
                        ins = pe.matmul(dst, a, b, start=first and n == 0,
                                        stop=(k == KT - 1 and n == 2), skip_group_check=True)
                return ins

            def sum_mod(m, tiles):
                pe.wait_ge(mod_comb, m + (QUARTERS + 1))
                for t in range(tiles):
                    ins = pe.matmul(mod_ps[:, t:t + 1], mod_acc[:, 0, 0, t * P:(t + 1) * P], ones[:],
                                    start=True, stop=True)
                ins.then_inc(mod_sums, 1)

            pe.wait_ge(consts, 10)
            pe.wait_ge(turned_out, 2 + TT * NG)

            for r in range(QUARTERS):
                pe.wait_ge(mod_comb, r + 1)
                for t in range(2 * GT):
                    ins = pe.matmul(mod_ps[:, t:t + 1], mod_acc[:, 0, t // GT, (t % GT) * P:(t % GT + 1) * P],
                                    ones[:], start=True, stop=True)
                ins.then_inc(mod_sums, 1)
                for n in range(QW):
                    g, jj = n // 2, n % 2
                    pe.wait_ge(h_done, GT * r + CK * (jj + 1))
                    pe.wait_ge(raw_used, CREDIT_RAW + QC * r + QM + n + 1)
                    for kk in range(CK):
                        k = GT * r + CK * jj + kk
                        wh, wl = w_high[:, n % SLOTS, kk, :], w_low[:, n % SLOTS, kk, :]
                        ins = tile_row(g, k, wh, wl, h_high, h_low)
                    ins.then_inc(chunk_mult, 1)

            def group(w, par, high, low, ready, tokens=False, between=None):
                pe.wait_ge(banks_free, w + 1)
                for j in range(NCH):
                    ready(j)
                    pe.wait_ge(raw_used, w * NCH + (PRE * NCH + CREDIT_RAW + j + 1))
                    for kk in range(CK):
                        ins = tile_row(par, CK * j + kk, w_high[:, j % SLOTS, kk, :], w_low[:, j % SLOTS, kk, :],
                                       high, low, tokens)
                    ins.then_inc(chunk_mult, 1)
                    if between and j == SLOTS - 1:
                        between()

            def h_ready(n):
                return lambda j: pe.wait_ge(h_done, n * KT + CK * (j + 1))

            with pe.Fori(0, NG - OPEN // 2) as i:
                for par in range(2):
                    group(i * 2 + (W_QK + OPEN + par), par, h_high, h_low, h_ready(0))
                    sum_mod(i * 2 + (M_ATTN + par), STRIP_ATTN)
            with pe.Fori(0, NG // 2) as i:
                for par in range(2):
                    group(i * 2 + (W_V + par), par, h_high, h_low, h_ready(0), tokens=True)
                    sum_mod(i * 2 + (M_ATTN + 2 * NG - OPEN + par), STRIP_ATTN)

            pe.wait_ge(banks_free, CREDIT_BANKS + W_O)
            for s in range(HEADS + 3):
                if s < HEADS:
                    z = bank[s % 4]
                    if s >= 4:
                        pe.wait_ge(att_a, s - 3)
                    pe.matmul(z[:, 0:T], k_t[:, s, 0:P], q_t[:, s, :], start=True, stop=False,
                              skip_group_check=True)
                    pe.matmul(z[:, T:ZC], k_t[:, s, P:T], q_t[:, s, P:T], start=False, stop=True,
                              skip_group_check=True).then_inc(att_z, 1)
                if 2 <= s < HEADS + 2:
                    a = s - 2
                    z, m = bank[a % 4], sp[a % 3]
                    pe.wait_ge(att_spm, a + 1)
                    pe.matmul(z[:, 0:T], neg_tri[:], m[:, 0:T], start=False, stop=False, skip_group_check=True)
                    pe.matmul(z[:, P:T], neg_ones[:], m[:, T:ZC], start=False, stop=False, skip_group_check=True)
                    pe.matmul(z[:, T:ZC], neg_tri[:], m[:, T:ZC], start=False, stop=True,
                              skip_group_check=True).then_inc(att_cum, 1)
                if s >= 3:
                    o = s - 3
                    dst = bank[6 + o % 2]
                    pe.wait_ge(att_am, o + 1)
                    if o >= 2:
                        pe.wait_ge(att_lo, o - 1)
                    pe.matmul(dst[:, 0:T], v_tok[:, 0, o * P:(o + 1) * P], probs[:, o % 3, 0:T],
                              start=True, stop=False, skip_group_check=True)
                    pe.matmul(dst[:, P:T], v_tok[:, 1, o * P:(o + 1) * P], probs[:, o % 3, T:ZC],
                              start=False, stop=True, skip_group_check=True).then_inc(att_o, 1)
                if s in (2 * SUBS - 1, 4 * SUBS - 1):
                    sum_mod(M_ATTN + 3 * NG - OPEN + s // (2 * SUBS), STRIP_ATTN)

            def o_ready(j):
                pe.wait_ge(att_lo, CK * (j + 1))

            def tail(n, w0, high, low, ready, strips):
                def pivot():
                    pe.wait_ge(ln_s, 5 * (n + 1))
                    for a in range(2):
                        ins = pe.matmul(piv_ps[:, 0:T], pivot_of[:], t_pair[:, a, :], start=(a == 0), stop=(a == 1))
                    ins.then_inc(ln_piv, 1)

                for g in range(NG):
                    group(w0 + g, g % 2, high, low, ready, between=pivot if g == NG - 1 else None)
                    if strips:
                        sum_mod(strips[0] + g, strips[1])
                pe.wait_ge(ln_q, 5 * (n + 1))
                for a in range(2):
                    pe.matmul(var_ps[:, 0:T], mean_of[:], q_pair[:, a, :], start=(a == 0), stop=False)
                for m in range(KT - GT, KT):
                    pe.wait_ge(ln_t, n * KT + m + 1)
                    ins = pe.matmul(off_ps[:, 0:T], mean_of[:], y[:, m, :], start=(m == KT - GT), stop=(m == KT - 1))
                ins.then_inc(ln_off, 1)
                for m in range(GT):
                    pe.wait_ge(ln_sq, 7 * n + NG - 1 + m + 1)
                    ins = pe.matmul(var_ps[:, 0:T], mean_of[:], stage[:, 1, m, :], start=False, stop=(m == GT - 1))
                ins.then_inc(ln_var, 1)

            def mlp(layer):
                w0, s0 = W_MLP[layer], S_MLP[layer]
                steps = 2 * NG if layer == 0 else NG

                def up(f):
                    with pe.Fori(0, NG // 2) as i:
                        for par in range(2):
                            group(f * (2 * NG) + i * 2 + (w0 + par), par, h_high, h_low, h_ready(2 * layer + 1))
                            sum_mod(f * steps + i * 2 + (M_MLP[layer] + par), STRIP_W1)

                def hidden_ready(f):
                    return lambda j: pe.wait_ge(post_done, f * (2 * NG) + (CREDIT_STAGE + s0 + CK * j // GT + 1))

                with pe.Fori(0, FC - 1) as f:
                    up(f)
                    with pe.Fori(0, NG // 2) as i:
                        for par in range(2):
                            group(f * (2 * NG) + i * 2 + (w0 + NG + par), par, hid_high, hid_low, hidden_ready(f))
                            if layer == 0:
                                sum_mod(f * steps + i * 2 + (M_MLP[0] + NG + par), STRIP_W2)
                up(FC - 1)
                tail(2 * layer + 1, w0 + 2 * NG * FC - NG, hid_high, hid_low, hidden_ready(FC - 1),
                     None if layer else (M_CONV - NG, STRIP_W2))

            tail(0, W_O, h_high, h_low, o_ready, (M_ATTN + 3 * NG, STRIP_ATTN))
            mlp(0)
            with pe.Fori(0, 3 * NG // 2) as i:
                for par in range(2):
                    group(i * 2 + (W_CIN + par), par, h_high, h_low, h_ready(2))
                    sum_mod(i * 2 + (M_CONV + par), STRIP_CONV)

            def conv_ready(j):
                pe.wait_ge(post_done, CREDIT_STAGE + S_CONV + NG + CK * j // GT + 1)

            tail(2, W_COUT, hid_high, hid_low, conv_ready, (M_CONV + 3 * NG, STRIP_CONV))
            mlp(1)
            for b in range(NG):
                pe.wait_ge(h_act, 2 * DEPTH * KT + GT * (b + 1))
                for t in range(TT):
                    if b >= 2:
                        pe.wait_ge((out_c, out_v)[t], b - 1)
                    for m in range(GT):
                        ins = pe.transpose(bank[(TT * b + t) % 4][:, m * P:(m + 1) * P],
                                           stage[:, b % 2, m, t * P:(t + 1) * P], ident[:])
                    ins.then_inc(out_t, 1)


_INS = ["x", "c", "mod_w", "mod_b", "ln_g", "ln_b", "attn_w_qkv", "attn_w_o", "conv_w_in", "conv_w",
        "conv_b", "conv_w_out", "mlp_w1", "mlp_b1", "mlp_w2", "mlp_b2"]


def kernel(**inputs):
    import concourse.bacc as bacc
    from concourse.bass_utils import run_bass_kernel_spmd

    nc = bacc.Bacc("TRN2", target_bir_lowering=False, num_devices=1, dynamic_dma_scratch_size=1024)
    arrays, args = {}, []
    for name in _INS:
        a = np.ascontiguousarray(inputs[name])
        arrays[f"in_{name}"] = a
        args.append(nc.dram_tensor(f"in_{name}", a.shape, mybir.dt.from_np(a.dtype), kind="ExternalInput").ap())
    shape = inputs["x"].shape
    out = nc.dram_tensor("out", shape, F32, kind="ExternalOutput").ap()
    build_trunk(nc, *args, out)
    r = run_bass_kernel_spmd(nc, [arrays], core_ids=[0])
    return r.results[0]["out"]
```

```python
from contextlib import ExitStack

import numpy as np
import concourse.bass as bass
from concourse import mybir

F32 = mybir.dt.float32
F32R = mybir.dt.float32r
ALU = mybir.AluOpType
ACT = mybir.ActivationFunctionType
ds = bass.ds

P = 128
CREDIT_RAW = 8
CREDIT_SPLIT = 4
CREDIT_BANKS = 2
CREDIT_STAGE = 2
SHIFT_M, SCALE_M, GATE_M, SHIFT_F, SCALE_F, GATE_F = range(6)


def build_trunk(nc, x, c, mod_w, mod_b, ln_g, ln_b, attn_w_qkv, attn_w_o,
                conv_w_in, conv_w, conv_b, conv_w_out, mlp_w1, mlp_b1, mlp_w2, mlp_b2, out):
    _, T, D = x.shape
    DEPTH = mod_w.shape[0]
    FF = mlp_w1.shape[2]
    KT = D // P
    TT = T // P
    HEADS = KT
    GC = 512
    GT = GC // P
    NCH = 8
    CK = KT // NCH
    NG = D // GC
    FC = FF // D
    SLOTS = 4
    ALPHA = (2.0 * DEPTH) ** 0.25
    EPS = 1e-5
    ZSCALE = float(P) ** -0.5
    assert DEPTH == 2 and T == 2 * P and KT == 16 and conv_w.shape[1] == 3

    W_QK = 0
    W_V = W_QK + 2 * NG
    W_O = W_V + NG
    W_MLP = [W_O + NG, 0]
    W_CIN = W_MLP[0] + 2 * NG * FC
    W_COUT = W_CIN + 3 * NG
    W_MLP[1] = W_COUT + NG
    W_END = W_MLP[1] + 2 * NG * FC
    S_CONV = 2 * NG * FC - NG
    S_MLP = [0, S_CONV + 2 * NG]
    OPEN = 2
    QUARTERS = KT // GT
    QM = 2 * NCH
    QW = OPEN * NCH // QUARTERS
    QC = QM + QW
    PRE = QUARTERS * QC // NCH - OPEN
    MC0 = QUARTERS * QM
    MD0 = 2 * QUARTERS
    M_ATTN = 0
    M_MLP = [4 * NG, 0]
    M_CONV = M_MLP[0] + 2 * NG * FC
    M_MLP[1] = M_CONV + 4 * NG
    MODT = 6 * KT
    STRIP_ATTN = 3 * KT // (4 * NG)
    STRIP_W1 = KT // (NG * FC)
    STRIP_W2 = 3 * KT // (NG * FC)
    STRIP_CONV = 2 * KT // (4 * NG)
    STRIP_MAX = max(STRIP_ATTN, STRIP_W1, STRIP_W2, STRIP_CONV) * P
    SUBS = 4
    SK = KT // SUBS

    V_C, V_MODB, V_LNG = 0, KT, KT + DEPTH * MODT
    V_LNB = V_LNG + 2 * DEPTH * KT
    V_CW = V_LNB + 2 * DEPTH * KT
    V_CB = V_CW + 3 * KT
    V_B2 = V_CB + KT
    V_B1 = V_B2 + DEPTH * KT
    V_ALL = V_B1 + DEPTH * FF // P

    ctx = ExitStack()
    with ctx:
        def sb(name, shape, dt=F32):
            return ctx.enter_context(nc.sbuf_tensor(name, shape, dt))

        def sem(name):
            return ctx.enter_context(nc.semaphore(name))

        with ExitStack() as early:
            q_t = early.enter_context(nc.sbuf_tensor("q_t", [P, KT, T], F32))
            k_t = early.enter_context(nc.sbuf_tensor("k_t", [P, KT, T], F32))
            v_tok = early.enter_context(nc.sbuf_tensor("v_tok", [P, TT, D], F32))
        hid_high = sb("hid_high", [P, KT, T], F32R)
        hid_low = sb("hid_low", [P, KT, T], F32R)
        y = sb("y", [P, KT, T])
        tok = q_t[:, :, :].rearrange("p k t -> p (k t)").rearrange("p (t d) -> p t d", t=TT)

        res = sb("res", [P, KT, T])
        h_high = sb("h_high", [P, KT, T], F32R)
        h_low = sb("h_low", [P, KT, T], F32R)
        raw = sb("raw", [P, NCH, CK, GC])
        w_high = sb("w_high", [P, SLOTS, CK, GC], F32R)
        w_low = sb("w_low", [P, SLOTS, CK, GC], F32R)
        mod_raw = sb("mod_raw", [P, SUBS, SK, STRIP_MAX])
        mod_acc = sb("mod_acc", [P, 2, 2, GC])
        stage = sb("stage", [P, 2, GT, T])
        gated = sb("gated", [P, GT, T + 2])
        ZC = T + P
        sig_rows = stage[:, :, :, :].rearrange("p a g t -> p (a g t)")
        soft = [sig_rows[:, i * ZC:(i + 1) * ZC] for i in range(2)]
        sp = [sig_rows[:, (2 + i) * ZC:(3 + i) * ZC] for i in range(3)]
        probs = sb("probs", [P, 3, ZC])
        vrow = sig_rows[:, 0:5 * P].rearrange("p (b n) -> p b n", b=5)
        ln_pair = probs[:, :, :].rearrange("p a z -> p (a z)")
        t_pair = ln_pair[:, 0:2 * T].rearrange("p (a t) -> p a t", a=2)
        q_pair = ln_pair[:, 2 * T:4 * T].rearrange("p (a t) -> p a t", a=2)
        vec = sb("vec", [P, V_ALL])
        mod = sb("mod", [P, DEPTH * MODT])
        cond = sb("cond", [P, 2, KT])
        coef = sb("coef", [P, 2 * DEPTH, 6, KT])
        coef0 = sb("coef0", [P, KT])
        ident = sb("ident", [P, P])
        mean_of = sb("mean_of", [P, P])
        ones = sb("ones", [P, 1])
        neg_ones = sb("neg_ones", [P, P])
        neg_tri = sb("neg_tri", [P, P])
        zeros = sb("zeros", [P, T])
        pivot_of = sb("pivot_of", [P, P])
        ln_tmp = sb("ln_tmp", [P, 6, T])
        var_t, root_t, new_t, piv_t, off_t, off2_t = (ln_tmp[:, i, :] for i in range(6))
        GATE1, SC1, A_, B_, RES_A, RES_B = range(6)

        bank = [ctx.enter_context(nc.psum_tensor(f"bank{i}", [P, 512], F32)) for i in range(8)]
        mod_ps = bank[4]
        piv_ps, off_ps, var_ps = bank[5], bank[6], bank[7]
        z_ps = [bank[0], bank[5], bank[6], bank[7]]
        o_ps = [bank[2][:, 0:T], bank[3][:, 0:T]]
        LEAD = 3
        STEPS = HEADS + 3
        M_HEADS = 3 * NG - OPEN

        small_in = sem("small_in")
        x_in = sem("x_in")
        consts = sem("consts")
        raw_in = [sem(f"raw_in{j}") for j in range(NCH)]
        mod_in = [sem(f"mod_in{r}") for r in range(SUBS)]
        raw_used = sem("raw_used")
        high_done = sem("high_done")
        chunk_mult = sem("chunk_mult")
        banks_free = sem("banks_free")
        post_done = sem("post_done")
        hidden_high = sem("hidden_high")
        squared = sem("squared")
        mod_chain = sem("mod_chain")
        mod_sums = sem("mod_sums")
        mod_done = sem("mod_done")
        turned = sem("turned")
        turned_out = sem("turned_out")
        cond_act = sem("cond_act")
        cond_dve = sem("cond_dve")
        coefs = sem("coefs")
        h_act = sem("h_act")
        h_pool = sem("h_pool")
        h_last = sem("h_last")
        h_high_done = sem("h_high_done")
        h_done = sem("h_done")
        att_z, att_act, att_l = sem("att_z"), sem("att_act"), sem("att_l")
        att_sp, att_spm, att_cum = sem("att_sp"), sem("att_spm"), sem("att_cum")
        att_a, att_am, att_o = sem("att_a"), sem("att_am"), sem("att_o")
        att_hi, att_lo = sem("att_hi"), sem("att_lo")
        conv_step = sem("conv_step")
        conv_c = sem("conv_c")
        mod_comb = sem("mod_comb")
        ln_t = sem("ln_t")
        ln_base = sem("ln_base")
        ln_gated = sem("ln_gated")
        ln_s = sem("ln_s")
        ln_piv = sem("ln_piv")
        ln_u = sem("ln_u")
        ln_ub = sem("ln_ub")
        ln_sq = sem("ln_sq")
        ln_q = sem("ln_q")
        ln_off = sem("ln_off")
        ln_var = sem("ln_var")
        ln_rs = sem("ln_rs")
        ln_root = sem("ln_root")
        ln_y = sem("ln_y")
        ln_yp = sem("ln_yp")
        ln_x = sem("ln_x")
        res_done = sem("res_done")
        y_init = sem("y_init")
        out_w = sem("out_w")
        out_t = sem("out_t")
        out_c = sem("out_c")
        out_v = sem("out_v")
        out_dma = sem("out_dma")

        qkv_rows = attn_w_qkv[0].rearrange("(k p) n -> p k n", p=P)
        wo_rows = attn_w_o[0].rearrange("(k p) n -> p k n", p=P)
        cin_rows = conv_w_in[0].rearrange("(k p) n -> p k n", p=P)
        cout_rows = conv_w_out[0].rearrange("(k p) n -> p k n", p=P)
        w1_rows = [mlp_w1[i].rearrange("(k p) n -> p k n", p=P) for i in range(DEPTH)]
        w2_rows = [mlp_w2[i].rearrange("(k p) n -> p k n", p=P) for i in range(DEPTH)]
        mod_rows = [mod_w[i].rearrange("(k p) n -> p k n", p=P) for i in range(DEPTH)]

        def stage_tiles(m0, m1):
            return stage[:, (m0 // GT) % 2, m0 % GT:m0 % GT + m1 - m0, :]

        def out_tile(m):
            return stage_tiles(m, m + 1)[:, 0, :] if m < 2 * GT else res[:, m, :]

        h_gated = gated[:, :, 2:T + 2]

        block = ctx.enter_context(nc.Block())

        @block.sync
        def _(sp_):
            mod_units = mod_rows[0].rearrange("p k (u n) -> p k u n", n=D)
            for r in range(QUARTERS):
                for n in range(QC):
                    at = r * QC + n
                    slot = at % NCH
                    sp_.wait_ge(raw_used, at + 1)
                    if n < QM:
                        j, part = n // 2, 1 - n % 2
                        src = mod_units[:, CK * j:CK * (j + 1), part, r * GC:(r + 1) * GC]
                    else:
                        g, k = (n - QM) // 2, r * GT + CK * ((n - QM) % 2)
                        src = qkv_rows[:, k:k + CK, g * GC:(g + 1) * GC]
                    sp_.dma_start(raw[:, slot, :, :], src).then_inc(raw_in[slot], 16)

            def load_sub(strip, r):
                m, layer, tiles, t0 = strip
                sp_.wait_ge(mod_chain, m * KT + (MC0 - KT + SK * (r + 1)))
                sp_.dma_start(mod_raw[:, r, :, 0:tiles * P],
                              mod_rows[layer][:, SK * r:SK * (r + 1), ds(t0 * P, tiles * P)]
                              ).then_inc(mod_in[r], 16)

            def load_group(w, rows, k0, col, strip=None):
                for j in range(NCH):
                    sp_.wait_ge(raw_used, w * NCH + (PRE * NCH + j + 1))
                    sp_.dma_start(raw[:, j, :, :], rows[:, ds(k0 + CK * j, CK), ds(col, GC)]
                                  ).then_inc(raw_in[j], 16)
                    if strip and j >= NCH - SUBS:
                        load_sub(strip, j - (NCH - SUBS))

            def attn_strip(m):
                return (m + M_ATTN, 0, STRIP_ATTN, m * STRIP_ATTN + GATE_M * KT)

            with sp_.Fori(OPEN, 3 * NG) as g:
                load_group(g + W_QK, qkv_rows, 0, g * GC, attn_strip(g - OPEN))
            load_group(W_O, wo_rows, 0, 0)
            for m in range(3 * NG - OPEN, 3 * NG + 1):
                for r in range(SUBS):
                    load_sub(attn_strip(m), r)
            with sp_.Fori(1, NG) as g:
                load_group(g + W_O, wo_rows, 0, g * GC, attn_strip(g + 3 * NG))

            def load_mlp(layer):
                w0, m0 = W_MLP[layer], M_MLP[layer]
                per = 2 * NG if layer == 0 else NG
                with sp_.Fori(0, FC) as f:
                    with sp_.Fori(0, NG) as g:
                        load_group(f * (2 * NG) + g + w0, w1_rows[layer], 0, f * D + g * GC,
                                   (f * per + g + m0, layer, STRIP_W1, f * NG + g + GATE_F * KT))
                    with sp_.Fori(0, NG) as g:
                        load_group(f * (2 * NG) + g + (w0 + NG), w2_rows[layer], f * KT, g * GC,
                                   None if layer else
                                   (f * per + g + (m0 + NG), 1, STRIP_W2, (f * NG + g) * STRIP_W2))

            load_mlp(0)
            for n, part in enumerate((1, 2, 0)):
                with sp_.Fori(0, NG) as g:
                    load_group(g + (W_CIN + n * NG), cin_rows, 0, g * GC + part * D,
                               (g + (M_CONV + n * NG), 1, STRIP_CONV,
                                g * STRIP_CONV + (SHIFT_F * KT + n * NG * STRIP_CONV)))
            with sp_.Fori(0, NG) as g:
                load_group(g + W_COUT, cout_rows, 0, g * GC,
                           (g + (M_CONV + 3 * NG), 1, STRIP_CONV,
                            g * STRIP_CONV + (SHIFT_F * KT + 3 * NG * STRIP_CONV)))
            load_mlp(1)
            o_rows = out[0].rearrange("(t p) d -> p t d", p=P)
            for b in range(NG):
                for t in range(TT):
                    sp_.wait_ge((out_c, out_v)[t], b + 1)
                    sp_.dma_start(o_rows[:, t, b * GC:(b + 1) * GC], tok[:, t, b * GC:(b + 1) * GC]
                                  ).then_inc(out_dma, 16)
            sp_.wait_ge(out_dma, 16 * NG * TT)

        @block.gpsimd
        def _(pool):
            pool.memset(ident[:], 0.0).then_inc(consts, 1)
            pool.memset(neg_tri[:], -1.0).then_inc(consts, 1)
            pool.memset(neg_ones[:], -1.0).then_inc(consts, 1)
            pool.memset(mean_of[:], 1.0 / D).then_inc(consts, 1)
            pool.memset(ones[:], 1.0).then_inc(consts, 1)
            pool.memset(zeros[:], 0.0).then_inc(consts, 1)
            pool.memset(gated[:, :, 0:2], 0.0).then_inc(consts, 1)
            pool.memset(pivot_of[:], 1.0 / (D - GC)).then_inc(consts, 1)
            pool.wait_ge(consts, 8)
            pool.affine_select(out=ident[:], in_=ident[:], compare_op=ALU.not_equal, fill=1.0, base=0,
                               pattern=[[-1, P]], channel_multiplier=1).then_inc(consts, 1)
            pool.affine_select(out=neg_tri[:], in_=neg_tri[:], compare_op=ALU.is_ge, fill=0.0, base=0,
                               pattern=[[-1, P]], channel_multiplier=1).then_inc(consts, 1)

            def causal(t, done):
                v = t.rearrange("p (b q) -> p b q", b=3)[:, 0:3:2, :]
                pool.affine_select(out=v, in_=v, compare_op=ALU.is_gt, fill=0.0, base=0,
                                   pattern=[[0, 2], [1, P]], channel_multiplier=-1).then_inc(done, 1)

            for s in range(HEADS + 2):
                if s < HEADS:
                    pool.wait_ge(att_sp, s + 1)
                    causal(sp[s % 3], att_spm)
                if s >= 2:
                    pool.wait_ge(att_a, s - 1)
                    causal(probs[:, (s - 2) % 3, :], att_am)

            n_coef = [0]

            def step(ins):
                n_coef[0] += 1
                ins.then_inc(coefs, 1)
                pool.wait_ge(coefs, n_coef[0])

            def gate_coefficient(n):
                layer, half = n // 2, n % 2
                gate = layer * MODT + (GATE_F if half else GATE_M) * KT
                step(pool.tensor_scalar(coef[:, n, GATE1], mod[:, gate:gate + KT], 1.0, 1.0, ALU.add, ALU.mult))

            def residual_sums(n):
                mlp = n % 2 == 1
                if mlp:
                    pool.wait_ge(res_done, n * KT)
                    pool.wait_ge(post_done, CREDIT_STAGE + S_MLP[n // 2] + 2 * NG * (FC - 1))
                    for m in range(KT):
                        pool.tensor_scalar(y[:, m, :], y[:, m, :], coef[:, n, GATE1, m:m + 1], 1.0,
                                           ALU.mult, ALU.mult).then_inc(ln_gated, 1)
                        pool.wait_ge(ln_gated, (n // 2) * KT + m + 1)
                        pool.tensor_tensor(y[:, m, :], y[:, m, :], res[:, m, :], ALU.add).then_inc(ln_base, 1)
                for g in range(NG - 1):
                    pool.wait_ge(ln_t, n * KT + GT * (g + 1))
                    for a in range(2):
                        if g == 0 and a == 0:
                            continue
                        if g:
                            pool.wait_ge(ln_s, 5 * n + 2 * g + a - 1)
                        pool.tensor_tensor(t_pair, y[:, 0:2, :] if g == 0 else t_pair,
                                           y[:, GT * g + 2 * a:GT * g + 2 * a + 2, :], ALU.add
                                           ).then_inc(ln_s, 1)
                pool.wait_ge(ln_piv, 2 * n + 2)
                if mlp:
                    pool.wait_ge(ln_base, (n // 2 + 1) * KT)
                ts = slice(KT - GT, KT)
                pool.tensor_tensor(y[:, ts, :], (y if mlp else res)[:, ts, :],
                                   piv_t.unsqueeze(1).to_broadcast([P, GT, T]), ALU.subtract).then_inc(ln_ub, 1)

            def sum_squares(n):
                for k in range(3):
                    b, a = divmod(k + 1, 2)
                    pool.wait_ge(ln_sq, 7 * n + b + 1)
                    if k:
                        pool.wait_ge(ln_q, 5 * n + k)
                    pool.tensor_tensor(q_pair, q_pair if k else stage[:, 0, 0:2], stage[:, b, 2 * a:2 * a + 2],
                                       ALU.add).then_inc(ln_q, 1)

            def last_tiles(n):
                pool.wait_ge(ln_off, 3 * n + 3)
                pool.wait_ge(ln_sq, 7 * (n + 1))
                pool.wait_ge(ln_t, n * KT + KT)
                for m0 in (2 * GT, 3 * GT):
                    yt = y[:, m0:m0 + GT, :]
                    pool.tensor_tensor(yt, yt, off_t.unsqueeze(1).to_broadcast([P, GT, T]), ALU.subtract
                                       ).then_inc(ln_yp, 1)
                pool.wait_ge(ln_rs, 4 * n + 4)
                pool.wait_ge(ln_yp, 3 * n + 2)
                pool.tensor_tensor(yt, yt, root_t.unsqueeze(1).to_broadcast([P, GT, T]), ALU.mult).then_inc(ln_yp, 1)

            def coefficients(n):
                half = n % 2
                g = vec[:, V_LNG + n * KT:V_LNG + (n + 1) * KT]
                b = vec[:, V_LNB + n * KT:V_LNB + (n + 1) * KT]
                k = coef[:, n]
                nl = (n + 1) // 2
                sh = nl * MODT + (SHIFT_M if half else SHIFT_F) * KT
                sc = sh + KT
                step(pool.tensor_scalar(k[:, SC1], mod[:, sc:sc + KT], 1.0, 1.0, ALU.add, ALU.mult))
                step(pool.tensor_tensor(k[:, A_], k[:, SC1], g, ALU.mult))
                step(pool.tensor_tensor(k[:, B_], k[:, SC1], b, ALU.mult))
                step(pool.tensor_tensor(k[:, B_], k[:, B_], mod[:, sh:sh + KT], ALU.add))
                step(pool.tensor_scalar(k[:, RES_A], g, ALPHA, 0.0, ALU.mult, ALU.add))
                step(pool.tensor_scalar(k[:, RES_B], b, ALPHA, 0.0, ALU.mult, ALU.add))

            def residual(n):
                pool.wait_ge(ln_yp, 3 * n + 3)
                for m in range(KT - GT, KT):
                    pool.tensor_scalar(h_gated[:, m % GT, :], y[:, m, :], coef[:, n, A_, m:m + 1],
                                       coef[:, n, B_, m:m + 1], ALU.mult, ALU.add).then_inc(h_pool, 1)
                for m in range(KT):
                    pool.wait_ge(ln_x, n * KT + m + 1)
                    pool.tensor_scalar(res[:, m, :], y[:, m, :], coef[:, n, RES_A, m:m + 1],
                                       coef[:, n, RES_B, m:m + 1], ALU.mult, ALU.add).then_inc(res_done, 1)
                    if n % 2 == 0:
                        b2 = V_B2 + (n // 2) * KT + m
                        pool.wait_ge(h_act, (n + 1) * KT + max(m + 1, 2))
                        pool.wait_ge(res_done, n * KT + m + 1)
                        pool.tensor_scalar(y[:, m, :], zeros[:], vec[:, b2:b2 + 1], 1.0, ALU.add, ALU.mult
                                           ).then_inc(y_init, 1)

            gate_need = [KT // STRIP_ATTN + 1, M_CONV - NG, M_CONV, M_MLP[1] + NG * FC]
            need = [M_MLP[0], M_CONV, M_MLP[1]]
            for n in range(2 * DEPTH):
                pool.wait_ge(mod_done, MD0 + gate_need[n])
                gate_coefficient(n)
                residual_sums(n)
                sum_squares(n)
                if n < 2 * DEPTH - 1:
                    pool.wait_ge(mod_done, MD0 + need[n])
                    coefficients(n)
                last_tiles(n)
                if n < 2 * DEPTH - 1:
                    residual(n)

        GATE_DONE = [7 * n + 1 for n in range(2 * DEPTH)]
        COEF_DONE = [7 * n + 7 for n in range(2 * DEPTH - 1)]
        BLOCKS = [(0, 1), (1, 2), (2, 4), (4, 6), (6, 8), (8, 12)]

        def counted(m0, m1):
            return m1 - m0 + (GT if m1 == KT - GT else 0)

        @block.scalar
        def _(act):
            batches = [
                [c.rearrange("b (k p) -> (b k) p", p=P), mod_b[0].rearrange("(k p) -> k p", p=P)],
                [mod_b[1].rearrange("(k p) -> k p", p=P)],
                [ln_g.rearrange("i j (k p) -> (i j k) p", p=P), ln_b.rearrange("i j (k p) -> (i j k) p", p=P)],
                [conv_w.rearrange("i w (k p) -> (i w k) p", p=P), conv_b.rearrange("i (k p) -> (i k) p", p=P),
                 mlp_b2.rearrange("i (k p) -> (i k) p", p=P)],
                [mlp_b1.rearrange("i (k p) -> (i k) p", p=P)],
            ]
            for b, parts in enumerate(batches):
                row = 0
                for part in parts:
                    n = part.shape[0]
                    act.dma_start(vrow[row:row + n, b, :], part).then_inc(small_in, 16)
                    row += n
            act.dma_start(tok[:, :, :], x[0].rearrange("(t p) d -> p t d", p=P)).then_inc(x_in, 16)
            act.preload_act_table_set("natural_log_exp_and_others")
            act.nop().then_inc(banks_free, CREDIT_BANKS)
            act.wait_ge(turned, 5)
            act.activation(vec[:, 0:V_CW], bank[7][:, 0:V_CW], ACT.Copy).then_inc(turned_out, 1)
            act.activation(vec[:, V_CW:V_ALL], bank[6][:, 0:V_ALL - V_CW], ACT.Copy).then_inc(turned_out, 1)
            act.wait_ge(turned_out, 1)
            act.activation(cond[:, 0, :], vec[:, V_C:V_C + KT], ACT.Exp, scale=-1.0).then_inc(cond_act, 1)
            for b in range(TT * NG):
                t, g = b // NG, b % NG
                act.wait_ge(turned, 5 + b + 1)
                act.activation(res[:, GT * g:GT * (g + 1), t * P:(t + 1) * P],
                               bank[b % 4][:, :].rearrange("p (k t) -> p k t", k=GT), ACT.Copy,
                               scale=ALPHA).then_inc(turned_out, 1)

            def high(w, j):
                act.wait_ge(raw_in[j], (w + PRE) * 16 + 16)
                act.wait_ge(chunk_mult, w * NCH + (j + 1))
                act.activation(w_high[:, j % SLOTS], raw[:, j], ACT.Copy).then_inc(high_done, 1)

            def highs(w):
                for j in range(SLOTS, NCH):
                    high(w, j)
                for j in range(SLOTS):
                    high(w + 1, j)
                act.wait_ge(chunk_mult, w * NCH + (CREDIT_SPLIT + NCH))

            def make_h(n, after):
                act.wait_ge(coefs, COEF_DONE[n - 1])
                for m0, m1 in BLOCKS:
                    act.wait_ge(ln_x, (n - 1) * KT + m1)
                    if m0 == 2 * GT:
                        act.wait_ge(h_pool, n * GT)
                        act.activation(h_high[:, KT - GT:KT, :], h_gated, ACT.Copy).then_inc(h_last, 1)
                        act.wait_ge(h_done, n * KT + m1 - 2 * GT)
                    else:
                        act.wait_ge(ln_var, n)
                    for m in range(m0, m1):
                        if m != 1:
                            act.activation(stage_tiles(m, m + 1)[:, 0, :], y[:, m, :], ACT.Identity,
                                           scale=coef[:, n - 1, A_, m:m + 1], bias=coef[:, n - 1, B_, m:m + 1]
                                           ).then_inc(h_act, 1 + GT if m == KT - GT - 1 else 1)
                    act.wait_ge(h_act, n * KT + (KT if m0 == 2 * GT else max(m1, 2)))
                    act.activation(h_high[:, m0:m1, :], stage_tiles(m0, m1), ACT.Copy
                                   ).then_inc(h_high_done, counted(m0, m1))
                    if m0 in (2, 4):
                        high(after, 1 + m0 // 2)

            act.wait_ge(turned_out, 2 + TT * NG)
            with act.Fori(0, QUARTERS // 2) as i:
                for q in range(2):
                    for n in range(QW):
                        at = q * QC + QM + n
                        act.wait_ge(raw_in[at % NCH], i * (16 * 2 * QC // NCH) + 16 * (at // NCH + 1))
                        act.wait_ge(chunk_mult, i * (2 * QW) + (q * QW + n + 1))
                        act.activation(w_high[:, n % SLOTS], raw[:, at % NCH], ACT.Copy).then_inc(high_done, 1)
                    act.wait_ge(cond_dve, i * 2 + (q + 4))
                    for m in range(GT):
                        t = i * (2 * GT) + (q * GT + m)
                        act.activation(stage[:, q, m, :], res[:, ds(t, 1), :].rearrange("p k t -> p (k t)"),
                                       ACT.Identity, scale=coef0[:, ds(t, 1)], bias=mod[:, ds(t, 1)]
                                       ).then_inc(h_act, 1)
                    act.wait_ge(h_act, i * (2 * GT) + (q + 1) * GT)
                    act.activation(h_high[:, ds(i * (2 * GT) + q * GT, GT), :], stage[:, q], ACT.Copy
                                   ).then_inc(h_high_done, GT)
            for j in range(SLOTS):
                high(OPEN, j)
            act.wait_ge(chunk_mult, OPEN * NCH + CREDIT_SPLIT)

            def empty(w, par, dst, scale=1.0, inc=banks_free):
                act.activation(dst(0), bank[2 * par][:, :], ACT.Copy, scale=scale)
                act.activation(dst(1), bank[2 * par + 1][:, :], ACT.Copy, scale=scale).then_inc(banks_free, 1)

            def to_tiles(t, g):
                return lambda b: t[:, ds(g * GT + 2 * b, 2), :].rearrange("p k t -> p (k t)")

            for g in range(OPEN):
                empty(None, g, to_tiles(q_t, g), ZSCALE)
            for g in range(OPEN, NG):
                highs(W_QK + g)
                empty(None, g % 2, to_tiles(q_t, g), ZSCALE)
            with act.Fori(0, NG // 2) as i:
                for par in range(2):
                    highs(i * 2 + (W_QK + NG + par))
                    empty(None, par, to_tiles(k_t, i * 2 + par))
            def soft_log(s):
                e = soft[s % 2]
                act.wait_ge(att_z, s + 1)
                if s >= 2:
                    act.wait_ge(att_sp, s - 1)
                act.activation(e, z_ps[s % 4][:, 0:ZC], ACT.Abs).then_inc(att_act, 1)
                act.wait_ge(att_act, 2 * s + 1)
                act.activation(e, e, ACT.Exp, scale=-1.0).then_inc(att_act, 1)
                act.wait_ge(att_act, 2 * s + 2)
                act.activation(e, e, ACT.Ln, bias=1.0).then_inc(att_l, 1)

            for g in range(NG):
                if g < NG - 1:
                    highs(W_V + g)
                else:
                    for j in range(SLOTS, NCH):
                        high(W_V + g, j)
                    for s in range(LEAD):
                        soft_log(s)
                    for j in range(SLOTS):
                        high(W_O, j)
                    act.wait_ge(chunk_mult, W_O * NCH + CREDIT_SPLIT)
                empty(None, g % 2, lambda b: v_tok[:, b, g * GC:(g + 1) * GC])

            for s in range(2, HEADS + 2):
                if LEAD <= s < HEADS:
                    soft_log(s)
                a = s - 2
                act.wait_ge(att_cum, a + 1)
                if a >= 3:
                    act.wait_ge(att_o, a - 2)
                act.activation(probs[:, a % 3, :], z_ps[a % 4][:, 0:ZC], ACT.Exp).then_inc(att_a, 1)

            def tail(n, w0):
                for g in range(NG):
                    if g < NG - 1:
                        highs(w0 + g)
                        act.wait_ge(ln_t, n * KT + GT * (g + 1))
                        act.nop().then_inc(banks_free, 1)
                        continue
                    for j in range(SLOTS, NCH):
                        high(w0 + g, j)
                    act.wait_ge(ln_piv, 2 * n + 1)
                    act.activation(piv_t, piv_ps[:, 0:T], ACT.Copy).then_inc(ln_piv, 1)
                    for b in range(NG - 1):
                        act.wait_ge(ln_u, (NG - 1) * n + b + 1)
                        if b >= 2:
                            act.wait_ge(ln_q, 5 * n + 1)
                        act.activation(stage[:, b % 2], y[:, GT * b:GT * (b + 1), :], ACT.Square
                                       ).then_inc(ln_sq, 1)
                    if n < 2 * DEPTH - 1:
                        high(w0 + NG, 0)
                    act.wait_ge(ln_q, 5 * n + 3)
                    for m in range(KT - GT, KT):
                        act.wait_ge(ln_t, n * KT + m + 1)
                        act.activation(stage[:, 1, m % GT, :], y[:, m, :], ACT.Square).then_inc(ln_sq, 1)
                    act.nop().then_inc(banks_free, 1)
                act.wait_ge(ln_off, 3 * n + 1)
                act.activation(off2_t, off_ps[:, 0:T], ACT.Square).then_inc(ln_off, 1)
                act.activation(off_t, off_ps[:, 0:T], ACT.Copy).then_inc(ln_off, 1)
                if n < 2 * DEPTH - 1:
                    high(w0 + NG, 1)
                act.wait_ge(ln_rs, 4 * n + 1)
                act.activation(root_t, var_t, ACT.Ln).then_inc(ln_root, 1)
                act.wait_ge(ln_root, 2 * n + 1)
                act.activation(root_t, root_t, ACT.Exp, scale=-0.5).then_inc(ln_root, 1)
                if n < 2 * DEPTH - 1:
                    make_h(n + 1, w0 + NG)

            def hidden_group(layer, f, g, par):
                w = f * (2 * NG) + g + W_MLP[layer]
                highs(w)
                act.wait_ge(post_done, f * (2 * NG) + g + (S_MLP[layer] + 1))
                b1 = V_B1 + layer * (FF // P)
                for m in range(GT):
                    ins = act.activation(stage[:, par, m, :], bank[2 * par + m // 2][:, T * (m % 2):T * (m % 2 + 1)],
                                         ACT.Relu, bias=vec[:, ds(f * KT + g * GT + (b1 + m), 1)])
                ins.then_inc(banks_free, 1)
                act.wait_ge(banks_free, w + (CREDIT_BANKS + 1))
                act.activation(stage[:, par], stage[:, par], ACT.Square).then_inc(squared, 1)
                act.wait_ge(squared, f * NG + g + (layer * NG * FC + 1))
                act.activation(hid_high[:, ds(g * GT, GT), :], stage[:, par], ACT.Copy).then_inc(hidden_high, 1)

            def down_group(layer, f, g, par):
                w = f * (2 * NG) + g + (W_MLP[layer] + NG)
                highs(w)
                act.wait_ge(post_done, f * (2 * NG) + g + (S_MLP[layer] + NG + 1))
                empty(None, par, lambda b: stage[:, par, 2 * b:2 * b + 2, :].rearrange("p k t -> p (k t)"))

            def mlp_up(layer, f):
                with act.Fori(0, NG // 2) as i:
                    for par in range(2):
                        hidden_group(layer, f, i * 2 + par, par)

            def mlp(layer):
                with act.Fori(0, FC - 1) as f:
                    mlp_up(layer, f)
                    with act.Fori(0, NG // 2) as i:
                        for par in range(2):
                            down_group(layer, f, i * 2 + par, par)
                mlp_up(layer, FC - 1)
                tail(2 * layer + 1, W_MLP[layer] + 2 * NG * FC - NG)

            tail(0, W_O)
            mlp(0)
            act.wait_ge(res_done, 2 * KT)
            with act.Fori(0, NG // 2) as i:
                for par in range(2):
                    highs(i * 2 + (W_CIN + par))
                    empty(None, par, to_tiles(y, i * 2 + par))
            with act.Fori(0, NG) as i:
                for par in range(2):
                    highs(i * 2 + (W_CIN + NG + par))
                    act.wait_ge(post_done, i * 2 + (S_CONV + par + 1))
                    empty(None, par, lambda b: stage[:, par, 2 * b:2 * b + 2, :].rearrange("p k t -> p (k t)"))
            tail(2, W_COUT)
            mlp(1)
            n = 2 * DEPTH - 1

            def rows_out(b):
                act.wait_ge(out_t, b + 1)
                act.activation(tok[:, 0, b * GC:(b + 1) * GC], bank[TT * b][:, :], ACT.Copy
                               ).then_inc(out_c, 1)

            act.wait_ge(ln_var, n + 1)
            for m in range(2 * GT):
                act.wait_ge(ln_x, n * KT + m + 1)
                act.activation(out_tile(m), y[:, m, :], ACT.Identity,
                               scale=vec[:, V_LNG + n * KT + m:V_LNG + n * KT + m + 1],
                               bias=vec[:, V_LNB + n * KT + m:V_LNB + n * KT + m + 1]).then_inc(h_act, 1)
            for b in range(NG - 1):
                rows_out(b)
            rows_out(NG - 1)

        @block.vector
        def _(dve):
            dve.nop().then_inc(raw_used, CREDIT_RAW)
            dve.nop().then_inc(post_done, CREDIT_STAGE)
            dve.wait_ge(cond_act, 1)
            dve.tensor_scalar(cond[:, 0, :], cond[:, 0, :], 1.0, None, ALU.add).then_inc(cond_dve, 1)
            dve.wait_ge(cond_dve, 1)
            dve.reciprocal(cond[:, 0, :], cond[:, 0, :]).then_inc(cond_dve, 1)
            dve.wait_ge(cond_dve, 2)
            dve.wait_ge(turned_out, 2)
            dve.tensor_tensor(cond[:, 1, :], cond[:, 0, :], vec[:, V_C:V_C + KT], ALU.mult).then_inc(cond_dve, 1)
            dve.wait_ge(cond_dve, 3)

            def add_rows(m, k, rows, cols, part=0):
                acc = mod_acc[:, k % 2, part, 0:cols]
                if k < 2:
                    dve.tensor_scalar(acc, rows, cond[:, 1, k:k + 1], None, ALU.mult).then_inc(mod_chain, 1)
                else:
                    dve.wait_ge(mod_chain, m * KT + (MC0 + k - 1))
                    dve.scalar_tensor_tensor(out=acc, in0=rows, scalar=cond[:, 1, k:k + 1], in1=acc,
                                             op0=ALU.mult, op1=ALU.add).then_inc(mod_chain, 1)

            def add_sub(m, r, tiles):
                dve.wait_ge(mod_in[r], m * 16 + 16)
                for k in range(SK):
                    add_rows(m, SK * r + k, mod_raw[:, r, k, 0:tiles * P], tiles * P)

            def combine(m, tiles, part=0):
                dve.wait_ge(mod_chain, m * KT + (MC0 + KT))
                dve.tensor_tensor(mod_acc[:, 0, part, 0:tiles * P], mod_acc[:, 0, part, 0:tiles * P],
                                  mod_acc[:, 1, part, 0:tiles * P], ALU.add).then_inc(mod_comb, 1)

            def write_mod(m, tile, tiles):
                dve.wait_ge(mod_sums, m + (QUARTERS + 1))
                dve.tensor_tensor(mod[:, ds(tile, tiles)], mod_ps[:, 0:tiles], vec[:, ds(tile + V_MODB, tiles)],
                                  ALU.add).then_inc(mod_done, 1)

            with dve.Fori(0, QUARTERS // 2) as i:
                for q in range(2):
                    r = i * 2 + q
                    for n in range(QM):
                        at = q * QC + n
                        j, part = n // 2, n % 2
                        dve.wait_ge(raw_in[at % NCH], i * (16 * 2 * QC // NCH) + 16 * (at // NCH + 1))
                        for k in range(CK):
                            acc = mod_acc[:, k, part, :]
                            rows = raw[:, at % NCH, k, :]
                            c1 = cond[:, 1, CK * j + k:CK * j + k + 1]
                            if j == 0:
                                ins = dve.tensor_scalar(acc, rows, c1, None, ALU.mult)
                            else:
                                if k == 0:
                                    dve.wait_ge(mod_chain, i * (2 * QM) + (q * QM + n - 1))
                                else:
                                    dve.wait_ge(raw_used, i * (2 * QC) + (CREDIT_RAW + at - 1))
                                ins = dve.scalar_tensor_tensor(out=acc, in0=rows, scalar=c1, in1=acc,
                                                               op0=ALU.mult, op1=ALU.add)
                            ins.then_inc(mod_chain if k == 0 else raw_used, 1)
                    dve.wait_ge(mod_chain, i * (2 * QM) + (q + 1) * QM)
                    dve.wait_ge(raw_used, i * (2 * QC) + (CREDIT_RAW + q * QC + QM))
                    dve.tensor_tensor(mod_acc[:, 0], mod_acc[:, 0], mod_acc[:, 1], ALU.add).then_inc(mod_comb, 1)
                    for n in range(QW):
                        at = q * QC + QM + n
                        dve.wait_ge(high_done, i * (2 * QW) + (q * QW + n + 1))
                        dve.tensor_tensor(w_low[:, n % SLOTS], raw[:, at % NCH], w_high[:, n % SLOTS].bitcast(F32),
                                          ALU.subtract).then_inc(raw_used, 1)
                    dve.wait_ge(mod_sums, r + 1)
                    for part, unit in ((0, SCALE_M), (1, SHIFT_M)):
                        dve.tensor_tensor(mod[:, ds(r * GT + unit * KT, GT)], mod_ps[:, GT * part:GT * (part + 1)],
                                          vec[:, ds(r * GT + (V_MODB + unit * KT), GT)], ALU.add
                                          ).then_inc(mod_done, 1)
                    dve.wait_ge(mod_done, i * 4 + 2 * (q + 1))
                    dve.tensor_scalar(coef0[:, ds(r * GT, GT)], mod[:, ds(r * GT + SCALE_M * KT, GT)], 1.0,
                                      1.0 / ALPHA, ALU.add, ALU.mult).then_inc(cond_dve, 1)
                    dve.wait_ge(h_high_done, i * (2 * GT) + (q + 1) * GT)
                    hs = ds(i * (2 * GT) + q * GT, GT)
                    dve.tensor_tensor(h_low[:, hs, :], stage[:, q], h_high[:, hs, :].bitcast(F32), ALU.subtract
                                      ).then_inc(h_done, GT)

            def low(w, j):
                dve.wait_ge(high_done, w * NCH + (j + 1))
                dve.tensor_tensor(w_low[:, j % SLOTS], raw[:, j], w_high[:, j % SLOTS].bitcast(F32),
                                  ALU.subtract).then_inc(raw_used, 1)

            def lows(w, strip=None, between=None):
                for j in range(SLOTS, NCH):
                    low(w, j)
                    if strip:
                        add_sub(strip[0], j - SLOTS, strip[1])
                if between:
                    between()
                for j in range(SLOTS):
                    low(w + 1, j)
                    if strip and j == 0:
                        combine(*strip)

            def low_h(n, m0, m1):
                dve.wait_ge(h_high_done, n * KT + m0 + counted(m0, m1))
                dve.tensor_tensor(h_low[:, m0:m1, :], stage_tiles(m0, m1), h_high[:, m0:m1, :].bitcast(F32),
                                  ALU.subtract).then_inc(h_done, counted(m0, m1))

            for j in range(SLOTS):
                low(OPEN, j)

            with dve.Fori(0, 3 * NG - OPEN - 1) as g:
                lows(g + (W_QK + OPEN), (g + M_ATTN, STRIP_ATTN))
                write_mod(g + M_ATTN, g * STRIP_ATTN + GATE_M * KT, STRIP_ATTN)

            def softplus(s):
                dve.wait_ge(att_l, s + 1)
                if s >= 3:
                    dve.wait_ge(att_cum, s - 2)
                dve.scalar_tensor_tensor(out=sp[s % 3], in0=z_ps[s % 4][:, 0:ZC], scalar=0.0,
                                         in1=soft[s % 2], op0=ALU.max, op1=ALU.add).then_inc(att_sp, 1)

            lows(W_O - 1, (M_HEADS - 1, STRIP_ATTN), lambda: [softplus(s) for s in range(LEAD)])
            write_mod(M_HEADS - 1, (M_HEADS - 1) * STRIP_ATTN + GATE_M * KT, STRIP_ATTN)

            for s in range(LEAD, STEPS):
                if s < HEADS:
                    softplus(s)
                o = s - 3
                dve.wait_ge(att_o, o + 1)
                dve.tensor_copy(h_high[:, o, :], o_ps[o % 2]).then_inc(att_hi, 1)
                m, k0 = divmod(2 * (s - LEAD), KT)
                dve.wait_ge(mod_in[k0 // SK], (M_HEADS + m) * 16 + 16)
                for k in (k0, k0 + 1):
                    add_rows(M_HEADS + m, k, mod_raw[:, k // SK, k % SK, 0:STRIP_ATTN * P], STRIP_ATTN * P, m)
                dve.wait_ge(att_hi, o + 1)
                dve.tensor_tensor(h_low[:, o, :], o_ps[o % 2], h_high[:, o, :].bitcast(F32),
                                  ALU.subtract).then_inc(att_lo, 1)
                if k0 + 2 == KT:
                    combine(M_HEADS + m, STRIP_ATTN, m)
                if s == STEPS // 2 + 5:
                    write_mod(M_HEADS, M_HEADS * STRIP_ATTN + GATE_M * KT, STRIP_ATTN)

            def layer_norm(n, after):

                def take_off(m0, m1):
                    yt = y[:, m0:m1, :]
                    dve.tensor_tensor(yt, yt, off_t.unsqueeze(1).to_broadcast([P, m1 - m0, T]), ALU.subtract
                                      ).then_inc(ln_y, 1)

                dve.wait_ge(ln_off, 3 * n + 3)
                dve.wait_ge(ln_u, (NG - 1) * (n + 1))
                take_off(0, 4)
                dve.wait_ge(ln_var, n + 1)
                dve.scalar_tensor_tensor(out=var_t, in0=var_ps[:, 0:T], scalar=EPS, in1=off2_t, op0=ALU.add,
                                         op1=ALU.subtract).then_inc(ln_rs, 1)
                take_off(4, 8)
                dve.wait_ge(ln_root, 2 * n + 2)
                dve.tensor_tensor(new_t, root_t, root_t, ALU.mult).then_inc(ln_rs, 1)
                dve.wait_ge(ln_rs, 4 * n + 2)
                dve.scalar_tensor_tensor(out=new_t, in0=new_t, scalar=-0.5, in1=var_t, op0=ALU.mult,
                                         op1=ALU.mult).then_inc(ln_rs, 1)
                dve.wait_ge(ln_rs, 4 * n + 3)
                dve.scalar_tensor_tensor(out=root_t, in0=new_t, scalar=1.5, in1=root_t, op0=ALU.add,
                                         op1=ALU.mult).then_inc(ln_rs, 1)
                dve.wait_ge(ln_rs, 4 * n + 4)

                def normalise(m0, m1):
                    if m0 < 2 * GT:
                        dve.wait_ge(ln_y, 2 * n + m0 // GT + 1)
                    else:
                        dve.wait_ge(ln_yp, 3 * n + 3)
                    yt = y[:, m0:m1, :]
                    dve.tensor_tensor(yt, yt, root_t.unsqueeze(1).to_broadcast([P, m1 - m0, T]), ALU.mult
                                      ).then_inc(ln_x, counted(m0, m1))

                for b in range(len(BLOCKS) + 1):
                    if b < len(BLOCKS):
                        normalise(*BLOCKS[b])
                    if after and b == 1:
                        dve.wait_ge(coefs, COEF_DONE[n])
                        dve.wait_ge(ln_x, n * KT + 2)
                        dve.tensor_scalar(stage_tiles(1, 2)[:, 0, :], y[:, 1, :], coef[:, n, A_, 1:2],
                                          coef[:, n, B_, 1:2], ALU.mult, ALU.add).then_inc(h_act, 1)
                    if after and b == len(BLOCKS):
                        dve.wait_ge(h_last, n + 1)
                        dve.tensor_tensor(h_low[:, KT - GT:KT, :], h_gated, h_high[:, KT - GT:KT, :].bitcast(F32),
                                          ALU.subtract)
                    if after and b:
                        for behind in {1: (0, 1), 2: ()}.get(b, (b - 1,)):
                            low_h(n + 1, *BLOCKS[behind])
                            if behind in (2, 3, 4):
                                low(after, behind - 1)

            def tail(n, w0, strips):
                mlp = n % 2 == 1
                base = y if mlp else res
                dve.wait_ge(coefs, GATE_DONE[n])
                if n:
                    dve.wait_ge(res_done, n * KT)
                if mlp:
                    dve.wait_ge(post_done, CREDIT_STAGE + S_MLP[n // 2] + 2 * NG * FC - NG)
                piv = piv_t.unsqueeze(1).to_broadcast([P, GT, T])
                for g in range(NG):
                    last = g == NG - 1
                    def pivot():
                        dve.wait_ge(ln_piv, 2 * n + 2)
                        for b in range(NG - 1):
                            ts = slice(GT * b, GT * (b + 1))
                            dve.tensor_tensor(y[:, ts, :], y[:, ts, :], piv, ALU.subtract).then_inc(ln_u, 1)

                    def strip_of_heads():
                        write_mod(M_HEADS + 1, (M_HEADS + 1) * STRIP_ATTN + GATE_M * KT, STRIP_ATTN)

                    if last:
                        for j in range(SLOTS, NCH):
                            low(w0 + g, j)
                            if strips:
                                add_sub(strips[0] + g, j - SLOTS, strips[1])
                        pivot()
                        if strips:
                            combine(strips[0] + g, strips[1])
                    else:
                        lows(w0 + g, strips and (strips[0] + g, strips[1]),
                             strip_of_heads if n == 0 and g == 0 else None)
                    dve.wait_ge(chunk_mult, (w0 + g) * NCH + (CREDIT_SPLIT + NCH))
                    if last:
                        dve.wait_ge(ln_ub, n + 1)
                    elif mlp:
                        dve.wait_ge(ln_base, (n // 2) * KT + GT * (g + 1))
                    for m in range(GT * g, GT * (g + 1)):
                        b = bank[2 * (g % 2) + (m % GT) // 2]
                        dve.scalar_tensor_tensor(out=y[:, m, :], in0=b[:, T * (m % 2):T * (m % 2 + 1)],
                                                 scalar=coef[:, n, GATE1, m:m + 1],
                                                 in1=(y if last else base)[:, m, :], op0=ALU.mult, op1=ALU.add
                                                 ).then_inc(ln_t, 1)
                    if strips:
                        write_mod(strips[0] + g, strips[2] + g * strips[1], strips[1])
                after = w0 + NG if n < 2 * DEPTH - 1 else None
                for a in range(2):
                    dve.wait_ge(ln_q, 5 * n + 3 + a)
                    dve.wait_ge(ln_sq, 7 * n + NG - 1)
                    dve.tensor_tensor(q_pair, q_pair, stage[:, 0, 2 * a:2 * a + 2], ALU.add).then_inc(ln_q, 1)
                if after:
                    low(after, 0)
                layer_norm(n, after)

            tail(0, W_O, (M_ATTN + 3 * NG, STRIP_ATTN, GATE_M * KT + 3 * NG * STRIP_ATTN))

            def hidden_group(layer, f, g, par):
                m = f * (2 * NG if layer == 0 else NG) + g + M_MLP[layer]
                lows(f * (2 * NG) + g + W_MLP[layer], (m, STRIP_W1))
                dve.wait_ge(hidden_high, f * NG + g + (layer * NG * FC + 1))
                dve.tensor_tensor(hid_low[:, ds(g * GT, GT), :], stage[:, par],
                                  hid_high[:, ds(g * GT, GT), :].bitcast(F32), ALU.subtract).then_inc(post_done, 1)
                write_mod(m, f * NG + g + (layer * MODT + GATE_F * KT), STRIP_W1)

            def down_group(layer, f, g, par):
                w = f * (2 * NG) + g + (W_MLP[layer] + NG)
                m = f * (2 * NG) + g + (M_MLP[layer] + NG)
                lows(w, (m, STRIP_W2) if layer == 0 else None)
                dve.wait_ge(banks_free, w + (CREDIT_BANKS + 1))
                dve.wait_ge(post_done, f * (2 * NG) + g + (CREDIT_STAGE + S_MLP[layer] + NG))
                yt = y[:, ds(g * GT, GT), :]
                dve.tensor_tensor(yt, yt, stage[:, par], ALU.add).then_inc(post_done, 1)
                if layer == 0:
                    write_mod(m, (f * NG + g) * STRIP_W2 + MODT, STRIP_W2)

            def mlp(layer):
                def up(f):
                    with dve.Fori(0, NG // 2) as i:
                        for par in range(2):
                            hidden_group(layer, f, i * 2 + par, par)

                with dve.Fori(0, FC - 1) as f:
                    up(f)
                    dve.wait_ge(y_init, (layer + 1) * KT)
                    with dve.Fori(0, NG // 2) as i:
                        for par in range(2):
                            down_group(layer, f, i * 2 + par, par)
                up(FC - 1)
                tail(2 * layer + 1, W_MLP[layer] + 2 * NG * FC - NG,
                     None if layer else (M_CONV - NG, STRIP_W2, MODT + (FC - 1) * NG * STRIP_W2))

            mlp(0)

            with dve.Fori(0, NG) as g:
                lows(g + W_CIN, (g + M_CONV, STRIP_CONV))
                write_mod(g + (M_CONV), g * STRIP_CONV + (MODT + SHIFT_F * KT), STRIP_CONV)
            with dve.Fori(0, NG // 2) as i:
                for par in range(2):
                    g = i * 2 + par
                    w = g + (W_CIN + NG)
                    lows(w, (g + (M_CONV + NG), STRIP_CONV))
                    dve.wait_ge(banks_free, w + (CREDIT_BANKS + 1))
                    dve.wait_ge(post_done, g + (CREDIT_STAGE + S_CONV))
                    dve.tensor_tensor(gated[:, :, 2:T + 2], stage[:, par], y[:, ds(g * GT, GT), :], ALU.mult
                                      ).then_inc(conv_step, 1)
                    steps = 1 + 2 * GT
                    for tap in (2, 1, 0):
                        for m in range(GT):
                            yt = y[:, ds(g * GT + m, 1), :].rearrange("p k t -> p (k t)")
                            cw = vec[:, ds(g * GT + (V_CW + tap * KT + m), 1)]
                            src = gated[:, m, tap:tap + T]
                            dve.wait_ge(conv_step, g * steps + (1 if tap == 2 else 1 + (1 - tap) * GT + m + 1))
                            if tap == 2:
                                dve.tensor_scalar(yt, src, cw, vec[:, ds(g * GT + (V_CB + m), 1)], ALU.mult,
                                                  ALU.add).then_inc(conv_step, 1)
                            else:
                                ins = dve.scalar_tensor_tensor(out=yt, in0=src, scalar=cw, in1=yt, op0=ALU.mult,
                                                               op1=ALU.add)
                                if tap == 1:
                                    ins.then_inc(conv_step, 1)
                    ins.then_inc(post_done, 1)
                    write_mod(g + (M_CONV + NG),
                              g * STRIP_CONV + (MODT + SHIFT_F * KT + NG * STRIP_CONV), STRIP_CONV)
            with dve.Fori(0, NG // 2) as i:
                for par in range(2):
                    g = i * 2 + par
                    w = g + (W_CIN + 2 * NG)
                    lows(w, (g + (M_CONV + 2 * NG), STRIP_CONV))
                    dve.wait_ge(banks_free, w + (CREDIT_BANKS + 1))
                    dve.wait_ge(post_done, g + (CREDIT_STAGE + S_CONV + NG))
                    st, hg = stage[:, par], hid_high[:, ds(g * GT, GT), :]
                    dve.tensor_tensor(st, st, y[:, ds(g * GT, GT), :], ALU.mult).then_inc(conv_c, 1)
                    dve.wait_ge(conv_c, g * 2 + 1)
                    dve.tensor_copy(hg, st).then_inc(conv_c, 1)
                    dve.wait_ge(conv_c, g * 2 + 2)
                    dve.tensor_tensor(hid_low[:, ds(g * GT, GT), :], st, hg.bitcast(F32), ALU.subtract
                                      ).then_inc(post_done, 1)
                    write_mod(g + (M_CONV + 2 * NG),
                              g * STRIP_CONV + (MODT + SHIFT_F * KT + 2 * NG * STRIP_CONV), STRIP_CONV)
            tail(2, W_COUT, (M_CONV + 3 * NG, STRIP_CONV, MODT + SHIFT_F * KT + 3 * NG * STRIP_CONV))
            mlp(1)
            n = 2 * DEPTH - 1
            dve.wait_ge(ln_x, (n + 1) * KT)
            for m in range(2 * GT, KT):
                dve.tensor_scalar(out_tile(m), y[:, m, :], vec[:, V_LNG + n * KT + m:V_LNG + n * KT + m + 1],
                                  vec[:, V_LNB + n * KT + m:V_LNB + n * KT + m + 1], ALU.mult, ALU.add
                                  ).then_inc(out_w, 1)
            for b in range(NG):
                dve.wait_ge(out_t, b + 1)
                dve.tensor_copy(tok[:, 1, b * GC:(b + 1) * GC], bank[TT * b + 1][:, :]).then_inc(out_v, 1)

        @block.tensor
        def _(pe):
            pe.nop().then_inc(chunk_mult, CREDIT_SPLIT)
            pe.wait_ge(consts, 9)
            pe.wait_ge(small_in, 16 * 9)
            rows = [KT + MODT, MODT, 4 * DEPTH * KT, 4 * KT + DEPTH * KT, DEPTH * FF // P]
            at = [0, KT + MODT, V_LNG, 0, V_B1 - V_CW]
            for b, n in enumerate(rows):
                dst = bank[7 if b < 3 else 6]
                pe.transpose(dst[:, at[b]:at[b] + n], vrow[0:n, b, :], ident[0:n, 0:n]).then_inc(turned, 1)
            pe.wait_ge(x_in, 16)
            for b in range(TT * NG):
                t, g = b // NG, b % NG
                if b >= 4:
                    pe.wait_ge(turned_out, 2 + b - 3)
                for m in range(GT):
                    ins = pe.transpose(bank[b % 4][:, m * P:(m + 1) * P],
                                       tok[:, t, (GT * g + m) * P:(GT * g + m + 1) * P], ident[:])
                ins.then_inc(turned, 1)

            def tile_row(par, k, wh, wl, high, low, tokens=False):
                for m in range(TT if tokens else GT):
                    s = slice(m * P, (m + 1) * P)
                    if tokens:
                        dst = bank[2 * par + m][:, :]
                        pairs = [(high[:, k, s], wh), (high[:, k, s], wl), (low[:, k, s], wh)]
                        first = k == 0
                    else:
                        dst = bank[2 * par + m // 2][:, T * (m % 2):T * (m % 2 + 1)]
                        pairs = [(wh[:, s], high[:, k, :]), (wh[:, s], low[:, k, :]), (wl[:, s], high[:, k, :])]
                        first = k == 0 and m % 2 == 0
                    for n, (a, b) in enumerate(pairs):
                        ins = pe.matmul(dst, a, b, start=first and n == 0,
                                        stop=(k == KT - 1 and n == 2), skip_group_check=True)
                return ins

            def sum_mod(m, tiles, part=0):
                pe.wait_ge(mod_comb, m + (QUARTERS + 1))
                for t in range(tiles):
                    ins = pe.matmul(mod_ps[:, t:t + 1], mod_acc[:, 0, part, t * P:(t + 1) * P], ones[:],
                                    start=True, stop=True)
                ins.then_inc(mod_sums, 1)

            pe.wait_ge(consts, 10)
            pe.wait_ge(turned_out, 2 + TT * NG)

            for r in range(QUARTERS):
                pe.wait_ge(mod_comb, r + 1)
                for t in range(2 * GT):
                    ins = pe.matmul(mod_ps[:, t:t + 1], mod_acc[:, 0, t // GT, (t % GT) * P:(t % GT + 1) * P],
                                    ones[:], start=True, stop=True)
                ins.then_inc(mod_sums, 1)
                for n in range(QW):
                    g, jj = n // 2, n % 2
                    pe.wait_ge(h_done, GT * r + CK * (jj + 1))
                    pe.wait_ge(raw_used, CREDIT_RAW + QC * r + QM + n + 1)
                    for kk in range(CK):
                        k = GT * r + CK * jj + kk
                        wh, wl = w_high[:, n % SLOTS, kk, :], w_low[:, n % SLOTS, kk, :]
                        ins = tile_row(g, k, wh, wl, h_high, h_low)
                    ins.then_inc(chunk_mult, 1)

            def group(w, par, high, low, ready, tokens=False, between=None):
                pe.wait_ge(banks_free, w + 1)
                for j in range(NCH):
                    ready(j)
                    pe.wait_ge(raw_used, w * NCH + (PRE * NCH + CREDIT_RAW + j + 1))
                    for kk in range(CK):
                        ins = tile_row(par, CK * j + kk, w_high[:, j % SLOTS, kk, :], w_low[:, j % SLOTS, kk, :],
                                       high, low, tokens)
                    ins.then_inc(chunk_mult, 1)
                    if between and j == SLOTS - 1:
                        between()

            def h_ready(n):
                return lambda j: pe.wait_ge(h_done, n * KT + CK * (j + 1))

            with pe.Fori(0, NG - OPEN // 2) as i:
                for par in range(2):
                    group(i * 2 + (W_QK + OPEN + par), par, h_high, h_low, h_ready(0))
                    sum_mod(i * 2 + (M_ATTN + par), STRIP_ATTN)
            def scores(s):
                z = z_ps[s % 4]
                if s >= 4:
                    pe.wait_ge(att_a, s - 3)
                pe.matmul(z[:, 0:T], k_t[:, s, 0:P], q_t[:, s, :], start=True, stop=False,
                          skip_group_check=True)
                pe.matmul(z[:, T:ZC], k_t[:, s, P:T], q_t[:, s, P:T], start=False, stop=True,
                          skip_group_check=True).then_inc(att_z, 1)

            def sums(a):
                z, m = z_ps[a % 4], sp[a % 3]
                pe.wait_ge(att_spm, a + 1)
                pe.matmul(z[:, 0:T], neg_tri[:], m[:, 0:T], start=False, stop=False, skip_group_check=True)
                pe.matmul(z[:, P:T], neg_ones[:], m[:, T:ZC], start=False, stop=False, skip_group_check=True)
                pe.matmul(z[:, T:ZC], neg_tri[:], m[:, T:ZC], start=False, stop=True,
                          skip_group_check=True).then_inc(att_cum, 1)

            def output(o):
                dst = o_ps[o % 2]
                pe.wait_ge(att_am, o + 1)
                if o >= 2:
                    pe.wait_ge(att_lo, o - 1)
                pe.matmul(dst, v_tok[:, 0, o * P:(o + 1) * P], probs[:, o % 3, 0:T],
                          start=True, stop=False, skip_group_check=True)
                pe.matmul(dst[:, P:T], v_tok[:, 1, o * P:(o + 1) * P], probs[:, o % 3, T:ZC],
                          start=False, stop=True, skip_group_check=True).then_inc(att_o, 1)

            def heads(s):
                if LEAD <= s < HEADS:
                    scores(s)
                if 2 <= s < HEADS + 2:
                    sums(s - 2)
                if s >= 3:
                    output(s - 3)

            def lead_scores():
                pe.wait_ge(banks_free, CREDIT_BANKS + W_O - 1)
                for s in range(LEAD):
                    scores(s)

            for g in range(NG):
                group(W_V + g, g % 2, h_high, h_low, h_ready(0), tokens=True,
                      between=lead_scores if g == NG - 1 else None)
                sum_mod(M_ATTN + 2 * NG - OPEN + g, STRIP_ATTN)

            pe.wait_ge(banks_free, CREDIT_BANKS + W_O)
            for s in range(2, STEPS - 2):
                heads(s)
                if s == STEPS // 2 + 3:
                    sum_mod(M_HEADS, STRIP_ATTN)

            def o_ready(j):
                pe.wait_ge(att_lo, CK * (j + 1))

            def o_ready_first(j):
                if j in (1, 2):
                    heads(STEPS - 3 + j)
                o_ready(j)

            def tail(n, w0, high, low, ready, strips):
                def pivot():
                    pe.wait_ge(ln_s, 5 * (n + 1))
                    for a in range(2):
                        ins = pe.matmul(piv_ps[:, 0:T], pivot_of[:], t_pair[:, a, :], start=(a == 0), stop=(a == 1))
                    ins.then_inc(ln_piv, 1)

                def strip_of_heads():
                    sum_mod(M_HEADS + 1, STRIP_ATTN, 1)

                for g in range(NG):
                    first = n == 0 and g == 0
                    group(w0 + g, g % 2, high, low, o_ready_first if first else ready,
                          between=pivot if g == NG - 1 else strip_of_heads if first else None)
                    if strips:
                        sum_mod(strips[0] + g, strips[1])
                for m in range(KT - GT, KT):
                    pe.wait_ge(ln_t, n * KT + m + 1)
                    ins = pe.matmul(off_ps[:, 0:T], mean_of[:], y[:, m, :], start=(m == KT - GT), stop=(m == KT - 1))
                ins.then_inc(ln_off, 1)
                for m in range(GT):
                    pe.wait_ge(ln_sq, 7 * n + NG - 1 + m + 1)
                    pe.matmul(var_ps[:, 0:T], mean_of[:], stage[:, 1, m, :], start=(m == 0), stop=False)
                pe.wait_ge(ln_q, 5 * (n + 1))
                for a in range(2):
                    ins = pe.matmul(var_ps[:, 0:T], mean_of[:], q_pair[:, a, :], start=False, stop=(a == 1))
                ins.then_inc(ln_var, 1)

            def mlp(layer):
                w0, s0 = W_MLP[layer], S_MLP[layer]
                steps = 2 * NG if layer == 0 else NG

                def up(f):
                    with pe.Fori(0, NG // 2) as i:
                        for par in range(2):
                            group(f * (2 * NG) + i * 2 + (w0 + par), par, h_high, h_low, h_ready(2 * layer + 1))
                            sum_mod(f * steps + i * 2 + (M_MLP[layer] + par), STRIP_W1)

                def hidden_ready(f):
                    return lambda j: pe.wait_ge(post_done, f * (2 * NG) + (CREDIT_STAGE + s0 + CK * j // GT + 1))

                with pe.Fori(0, FC - 1) as f:
                    up(f)
                    with pe.Fori(0, NG // 2) as i:
                        for par in range(2):
                            group(f * (2 * NG) + i * 2 + (w0 + NG + par), par, hid_high, hid_low, hidden_ready(f))
                            if layer == 0:
                                sum_mod(f * steps + i * 2 + (M_MLP[0] + NG + par), STRIP_W2)
                up(FC - 1)
                tail(2 * layer + 1, w0 + 2 * NG * FC - NG, hid_high, hid_low, hidden_ready(FC - 1),
                     None if layer else (M_CONV - NG, STRIP_W2))

            tail(0, W_O, h_high, h_low, o_ready, (M_ATTN + 3 * NG, STRIP_ATTN))
            mlp(0)
            with pe.Fori(0, 3 * NG // 2) as i:
                for par in range(2):
                    group(i * 2 + (W_CIN + par), par, h_high, h_low, h_ready(2))
                    sum_mod(i * 2 + (M_CONV + par), STRIP_CONV)

            def conv_ready(j):
                pe.wait_ge(post_done, CREDIT_STAGE + S_CONV + NG + CK * j // GT + 1)

            tail(2, W_COUT, hid_high, hid_low, conv_ready, (M_CONV + 3 * NG, STRIP_CONV))
            mlp(1)
            for b in range(NG):
                for m in range(GT * b, GT * (b + 1)):
                    if m < 2 * GT:
                        pe.wait_ge(h_act, (2 * DEPTH) * KT + m + 1)
                    else:
                        pe.wait_ge(out_w, m + 1 - 2 * GT)
                    for t in range(TT):
                        ins = pe.transpose(bank[TT * b + t][:, (m % GT) * P:(m % GT + 1) * P],
                                           out_tile(m)[:, t * P:(t + 1) * P], ident[:])
                ins.then_inc(out_t, 1)


_INS = ["x", "c", "mod_w", "mod_b", "ln_g", "ln_b", "attn_w_qkv", "attn_w_o", "conv_w_in", "conv_w",
        "conv_b", "conv_w_out", "mlp_w1", "mlp_b1", "mlp_w2", "mlp_b2"]


def kernel(**inputs):
    import concourse.bacc as bacc
    from concourse.bass_utils import run_bass_kernel_spmd

    nc = bacc.Bacc("TRN2", target_bir_lowering=False, num_devices=1, dynamic_dma_scratch_size=1024)
    arrays, args = {}, []
    for name in _INS:
        a = np.ascontiguousarray(inputs[name])
        arrays[f"in_{name}"] = a
        args.append(nc.dram_tensor(f"in_{name}", a.shape, mybir.dt.from_np(a.dtype), kind="ExternalInput").ap())
    shape = inputs["x"].shape
    out = nc.dram_tensor("out", shape, F32, kind="ExternalOutput").ap()
    build_trunk(nc, *args, out)
    r = run_bass_kernel_spmd(nc, [arrays], core_ids=[0])
    return r.results[0]["out"]
```
